# Optimizing a Trainium2 kernel written in Bass

```python
import math
import jax, jax.numpy as jnp
from jax import lax
import numpy as np

D_MODEL = 1024
BATCH = 1
SEQ = 512
DEPTH = 1

HEAD_DIM = 64
ATTN_GROUPS = ((128, 1), (512, 4), (2048, 16))
HEADS_PER_GROUP = 4
N_ATTN_HEADS = HEADS_PER_GROUP * len(ATTN_GROUPS)
ATTN_WIDTH = N_ATTN_HEADS * HEAD_DIM
ATTN_OUT_WIDTH = HEADS_PER_GROUP * HEAD_DIM
CONV_WIDTH = D_MODEL
CONV_K = 3
N_BUCKETS = 32
MAX_DISTANCE = 2048
N_EXPERTS = 32
TOP_K = 4
D_EXPERT = D_MODEL
SWIGLU_LIMIT = 7.0
SWIGLU_ALPHA = 1.702
MOE_BLOCK = 128
EPS = 1e-6
IN_SPLITS = (CONV_WIDTH, CONV_WIDTH, CONV_WIDTH, ATTN_WIDTH, ATTN_WIDTH, ATTN_WIDTH, D_MODEL, D_MODEL)
IN_WIDTH = sum(IN_SPLITS)
IN_CUTS = tuple(int(c) for c in np.cumsum(IN_SPLITS)[:-1])

kernel_name = "hybrid_gated_conv_dilated_attn_moe"

def rms_norm(x, g):
    xf = x.astype(jnp.float32)
    y = xf * lax.rsqrt(jnp.mean(xf * xf, axis=-1, keepdims=True) + EPS)
    return (y * g.astype(jnp.float32)).astype(x.dtype)

def t5_causal_bucket(dist):
    max_exact = N_BUCKETS // 2
    d = jnp.maximum(dist.astype(jnp.float32), 1.0)
    large = max_exact + (jnp.log(d / max_exact) / math.log(MAX_DISTANCE / max_exact)
                         * (N_BUCKETS - max_exact)).astype(jnp.int32)
    large = jnp.minimum(large, N_BUCKETS - 1)
    return jnp.where(dist < max_exact, dist, large)

def dilated_window_attention(q, k, v, rel_bias_g, window, dil):
    B, S, H, Dh = q.shape
    blk = window // dil
    L = -(-S // (dil * blk)) * blk
    pad = L * dil - S
    nblk = L // blk

    def to_blocks(t):
        t = jnp.pad(t, ((0, 0), (0, pad), (0, 0), (0, 0))).reshape(B, L, dil, H, Dh)
        return t.transpose(0, 2, 3, 1, 4).reshape(B, dil, H, nblk, blk, Dh)

    def with_prev(t):
        prev = jnp.pad(t, ((0, 0), (0, 0), (0, 0), (1, 0), (0, 0), (0, 0)))[:, :, :, :-1]
        return jnp.concatenate([prev, t], axis=4)

    qb = to_blocks(q)
    kw = with_prev(to_blocks(k))
    vw = with_prev(to_blocks(v))

    qi = jnp.arange(blk)[:, None]
    kj = jnp.arange(2 * blk)[None, :]
    delta = qi + blk - kj
    band = (delta >= 0) & (delta <= blk)
    valid = band[None] & ((jnp.arange(nblk)[:, None, None] > 0) | (kj[None] >= blk))
    bucket = t5_causal_bucket(jnp.clip(delta, 0, blk) * dil)
    bias = rel_bias_g[bucket].transpose(2, 0, 1).astype(jnp.float32)

    logits = jnp.einsum('brhnqd,brhnkd->brhnqk', qb, kw,
                        preferred_element_type=jnp.float32) * (Dh ** -0.5)
    logits = logits + bias[:, None]
    logits = jnp.where(valid, logits, -jnp.inf)
    m = jnp.max(logits, axis=-1, keepdims=True)
    p = jnp.exp(logits - m)
    s = jnp.sum(p, axis=-1, keepdims=True)
    o = jnp.einsum('brhnqk,brhnkd->brhnqd', p, vw.astype(jnp.float32)) / s
    lse = (m + jnp.log(s))[..., 0]

    o = o.reshape(B, dil, H, L, Dh).transpose(0, 3, 1, 2, 4).reshape(B, L * dil, H, Dh)[:, :S]
    lse = lse.reshape(B, dil, H, L).transpose(0, 3, 1, 2).reshape(B, L * dil, H)[:, :S]
    return o, lse

def token_mixer(h, w_in, q_norm_g, k_norm_g, rel_bias, conv_w, w_branch_conv, w_branch_attn, w_out):
    B, S, _ = h.shape
    proj = h @ w_in
    c_b, c_c, c_x, q, k, v, g_conv, g_attn = jnp.split(proj, IN_CUTS, axis=-1)

    u = c_c * c_x
    u = lax.conv_general_dilated(u, conv_w.reshape(CONV_K, 1, CONV_WIDTH).astype(u.dtype),
                                 window_strides=(1,), padding=[(CONV_K - 1, 0)],
                                 dimension_numbers=('NWC', 'WIO', 'NWC'),
                                 feature_group_count=CONV_WIDTH)
    y_conv = (c_b * u) @ w_branch_conv

    q = rms_norm(q.reshape(B, S, N_ATTN_HEADS, HEAD_DIM), q_norm_g)
    k = rms_norm(k.reshape(B, S, N_ATTN_HEADS, HEAD_DIM), k_norm_g)
    v = v.reshape(B, S, N_ATTN_HEADS, HEAD_DIM)
    outs, lses = [], []
    for gi, (window, dil) in enumerate(ATTN_GROUPS):
        hs = slice(gi * HEADS_PER_GROUP, (gi + 1) * HEADS_PER_GROUP)
        o_g, lse_g = dilated_window_attention(q[:, :, hs], k[:, :, hs], v[:, :, hs],
                                              rel_bias[:, hs], window, dil)
        outs.append(o_g)
        lses.append(lse_g)
    outs = jnp.stack(outs, axis=0)
    wts = jax.nn.softmax(jnp.stack(lses, axis=0), axis=0)
    o = jnp.sum(wts[..., None] * outs, axis=0).astype(h.dtype)
    y_attn = o.reshape(B, S, ATTN_OUT_WIDTH) @ w_branch_attn

    merged = jax.nn.sigmoid(g_conv) * y_conv + jax.nn.sigmoid(g_attn) * y_attn
    return merged @ w_out

def moe(h, w_router, b_router, w_gate_up, b_gate_up, w_down, b_down):
    B, S, D = h.shape
    T = B * S
    TK = T * TOP_K
    hf = h.reshape(T, D)
    logits = (hf @ w_router + b_router).astype(jnp.float32)
    top_vals, top_idx = lax.top_k(logits, TOP_K)
    gates = jax.nn.softmax(top_vals, axis=-1).astype(h.dtype)

    flat_e = top_idx.reshape(-1)
    flat_tok = jnp.arange(TK, dtype=jnp.int32) // TOP_K
    order = jnp.argsort(flat_e, stable=True)
    sorted_e = flat_e[order]
    sorted_tok = flat_tok[order]
    sorted_w = gates.reshape(-1)[order]

    counts = jax.ops.segment_sum(jnp.ones((TK,), jnp.int32), flat_e, num_segments=N_EXPERTS)
    start = jnp.cumsum(counts) - counts
    pcounts = (counts + MOE_BLOCK - 1) // MOE_BLOCK * MOE_BLOCK
    pend = jnp.cumsum(pcounts)
    poff = pend - pcounts
    dest = poff[sorted_e] + (jnp.arange(TK, dtype=jnp.int32) - start[sorted_e])

    p_max = TK + N_EXPERTS * MOE_BLOCK
    n_blocks = p_max // MOE_BLOCK
    row_tok = jnp.full((p_max,), T, jnp.int32).at[dest].set(sorted_tok)
    hp = jnp.concatenate([hf, jnp.zeros((1, D), hf.dtype)], axis=0)
    xs = hp[row_tok].reshape(n_blocks, MOE_BLOCK, D)
    block_e = jnp.clip(jnp.searchsorted(pend, jnp.arange(n_blocks) * MOE_BLOCK, side='right'),
                       0, N_EXPERTS - 1)

    def expert_block(args):
        xb, e = args
        gu = xb @ w_gate_up[e] + b_gate_up[e]
        gate, up = gu[:, :D_EXPERT], gu[:, D_EXPERT:]
        gate = jnp.minimum(gate, SWIGLU_LIMIT)
        up = jnp.clip(up, -SWIGLU_LIMIT, SWIGLU_LIMIT)
        act = (up + 1) * (gate * jax.nn.sigmoid(SWIGLU_ALPHA * gate))
        return act @ w_down[e] + b_down[e]

    ys = lax.map(expert_block, (xs, block_e)).reshape(p_max, D)
    y_assign = ys[dest] * sorted_w[:, None]
    out = jax.ops.segment_sum(y_assign, sorted_tok, num_segments=T)
    return out.reshape(B, S, D)

def setup_inputs(seed: int = 0) -> dict:
    key = jax.random.key(seed)
    ks = jax.random.split(key, 20)
    f32 = jnp.float32
    nrm = lambda k, shape, scale: jax.random.normal(k, shape, f32) * scale
    return {
        "x": nrm(ks[0], (BATCH, SEQ, D_MODEL), 1.0),
        "norm1_g": 1.0 + nrm(ks[1], (DEPTH, D_MODEL), 0.01),
        "w_in": nrm(ks[2], (DEPTH, D_MODEL, IN_WIDTH), D_MODEL ** -0.5),
        "q_norm_g": 1.0 + nrm(ks[3], (DEPTH, HEAD_DIM), 0.01),
        "k_norm_g": 1.0 + nrm(ks[4], (DEPTH, HEAD_DIM), 0.01),
        "rel_bias": nrm(ks[5], (N_BUCKETS, N_ATTN_HEADS), 0.1),
        "conv_w": nrm(ks[6], (DEPTH, CONV_K, CONV_WIDTH), CONV_K ** -0.5),
        "w_branch_conv": nrm(ks[7], (DEPTH, CONV_WIDTH, D_MODEL), CONV_WIDTH ** -0.5),
        "w_branch_attn": nrm(ks[8], (DEPTH, ATTN_OUT_WIDTH, D_MODEL), ATTN_OUT_WIDTH ** -0.5),
        "w_out": nrm(ks[9], (DEPTH, D_MODEL, D_MODEL), D_MODEL ** -0.5),
        "norm2_g": 1.0 + nrm(ks[10], (DEPTH, D_MODEL), 0.01),
        "w_router": nrm(ks[11], (DEPTH, D_MODEL, N_EXPERTS), D_MODEL ** -0.5),
        "b_router": nrm(ks[12], (DEPTH, N_EXPERTS), 0.01),
        "w_gate_up": nrm(ks[13], (DEPTH, N_EXPERTS, D_MODEL, 2 * D_EXPERT), D_MODEL ** -0.5),
        "b_gate_up": nrm(ks[14], (DEPTH, N_EXPERTS, 2 * D_EXPERT), 0.01),
        "w_down": nrm(ks[15], (DEPTH, N_EXPERTS, D_EXPERT, D_MODEL), D_EXPERT ** -0.5),
        "b_down": nrm(ks[16], (DEPTH, N_EXPERTS, D_MODEL), 0.01),
    }

def reference(x, norm1_g, w_in, q_norm_g, k_norm_g, rel_bias, conv_w, w_branch_conv,
              w_branch_attn, w_out, norm2_g, w_router, b_router, w_gate_up, b_gate_up,
              w_down, b_down):
    for l in range(DEPTH):
        h = rms_norm(x, norm1_g[l])
        x = x + token_mixer(h, w_in[l], q_norm_g[l], k_norm_g[l], rel_bias, conv_w[l],
                            w_branch_conv[l], w_branch_attn[l], w_out[l])
        h = rms_norm(x, norm2_g[l])
        x = x + moe(h, w_router[l], b_router[l], w_gate_up[l], b_gate_up[l],
                    w_down[l], b_down[l])
    return x


_drawn_inputs = setup_inputs


def setup_inputs(seed=0):
    import zlib

    import numpy as np

    out = dict(_drawn_inputs(seed))
    spreads = {}
    factors = {'q_norm_g': 6.342, 'k_norm_g': 8.0, 'rel_bias': 2.986, 'b_gate_up': 8.0, 'b_down': 8.0}
    for name, (base, spread) in spreads.items():
        noise = np.random.default_rng([zlib.crc32(name.encode()), seed]).standard_normal(out[name].shape)
        drawn = base * np.exp(spread * noise) if base else spread * noise
        out[name] = __import__('jax').numpy.asarray(drawn.astype(out[name].dtype))
    for name, factor in factors.items():
        out[name] = (out[name] * factor).astype(out[name].dtype)
    return out
```

```python
import math
from contextlib import ExitStack

import numpy as np

import concourse.bass as bass
from concourse import mybir

F32 = mybir.dt.float32
F32R = mybir.dt.float32r
BF16 = mybir.dt.bfloat16
U32 = mybir.dt.uint32
ALU = mybir.AluOpType
ACT = mybir.ActivationFunctionType
AX = mybir.AxisListType

P = 128
D = 1024
S = 512
NB = S // P
KD = D // P
DH = 64
HPG = 4
NG = 3
NH = HPG * NG
QT = NH * DH // P
AW = NH * DH
NE = 32
TOPK = 4
LIMIT = 7.0
ALPHA = 1.702
EPS = 1e-6
BUCKETS = 32
WINDOWS = ((128, 1), (512, 4), (2048, 16))
MAXDIST = 2048
NEG = -1e30
NSH = 2 * NB - 1
VEC = 2 * P

MAXOVER = S * TOPK // (P + 1)
MAXBLK = NE + MAXOVER
NCOL = MAXBLK + 1
OUT_OF_RANGE = 1 << 14

RAW = 3
UN = 4
XRAW, XUN = 6, 8
CH = 2048
UH = CH // 2
AHEAD = 3

C_ID, C_TRI, C_BLK, C_ONE, C_IOTA = 0, 128, 256, 384, 512
C_TOK, C_TOK4, C_RMOD = 640, 644, 648
C_END = 649


def constants():
    c = np.zeros((P, C_END), np.float32)
    p = np.arange(P)
    c[:, C_ID:C_ID + P] = np.eye(P)
    c[:, C_TRI:C_TRI + P] = p[:, None] < p[None, :]
    c[:, C_BLK:C_BLK + P] = (p[:, None] // DH == p[None, :] // DH) / DH
    c[:, C_ONE:C_ONE + P] = 1.0
    c[:, C_IOTA:C_IOTA + P] = p[None, :] + 1
    for b in range(NB):
        c[:, C_TOK + b] = NB * p + b - OUT_OF_RANGE
        c[:, C_TOK4 + b] = TOPK * (NB * p + b) - OUT_OF_RANGE
    c[:, C_RMOD] = p % NE + 1
    return c


def bucket(dist):
    exact = BUCKETS // 2
    d = np.maximum(dist.astype(np.float32), np.float32(1.0))
    large = exact + (np.log(d / np.float32(exact)) / np.float32(math.log(MAXDIST / exact))
                     * np.float32(BUCKETS - exact)).astype(np.int32)
    return np.where(dist < exact, dist, np.minimum(large, BUCKETS - 1))


def bucket_rows():
    n = np.arange(VEC) - (P - 1)
    rows = np.zeros((BUCKETS + 1, NSH + 2, VEC), np.float32)
    for v in range(NSH + 2):
        g = max(0, v - NSH + 1)
        window, dil = WINDOWS[g]
        dist = -NB * n + (NB - 1 - v if g == 0 else 0)
        ok = (dist >= 0) & (dist <= window) & (dist % dil == 0)
        rows[bucket(np.maximum(dist, 0)), v, np.arange(VEC)] = ok
        rows[BUCKETS, v] = np.where(ok, 0.0, NEG)
    return rows.reshape(BUCKETS + 1, -1)


def weight_chunks():
    order = [("q", i) for i in range(3)] + [("k", i) for i in range(3)] + [("v", i) for i in range(3)]
    for i in range(4):
        order += [("cc", i), ("cx", i), ("cb", i)]
    order += [("wba", 0)]
    for i in range(4):
        order += [("gc", i), ("wbc", i)]
    order += [("ga", i) for i in range(4)]
    order += [("wo", i) for i in range(4)]
    return order


CHUNKS = weight_chunks()
NF = len(CHUNKS)
UF = 2 * NF
CPE = 12
UPE = 2 * CPE
IN_COL = {"cb": 0, "cc": D, "cx": 2 * D, "q": 3 * D, "k": 3 * D + AW, "v": 3 * D + 2 * AW,
          "gc": 3 * D + 3 * AW, "ga": 4 * D + 3 * AW}
IN_WIDTH = 5 * D + 3 * AW
WAVE = {"q": 0, "k": 0}


def front_steps():
    steps, unit = [], 0

    def units(n):
        nonlocal unit
        for _ in range(n):
            steps.append(("unit", unit))
            unit += 1

    for c in range(6):
        units(1)
        if c:
            steps.extend([("ss", 2 * c - 2), ("ss", 2 * c - 1)])
        units(1)
    steps.extend([("ss", 10), ("ss", 11)])
    units(6)
    steps.extend([("S", 0), ("M", 0)])
    halves = [(kind, n) for n in range(unit, unit + 24) for kind in ("half", "unit")]
    unit += 24
    for u in range(HPG * NB):
        steps.extend(halves[3 * u:3 * u + 2])
        if u + 1 < HPG * NB:
            steps.append(("S", u + 1))
        steps.append(("T", u))
        if u + 1 < HPG * NB:
            steps.append(("M", u + 1))
        steps.append(halves[3 * u + 2])
        steps.append(("PV", u))
    units(UF - unit)
    return steps


STEPS = front_steps()


def tile_events():
    ev = [("xT", k, k, "dve") for k in range(KD)]
    t = 0
    for kind, n in STEPS:
        if kind == "ss":
            ev.append(("ss", n, 4 + n % 4, "act"))
        if kind != "unit":
            continue
        name, i = CHUNKS[n // 2]
        if name == "wba":
            ev += [("wba", 4 * (n % 2) + m, m, "act") for m in range(4)]
        elif n % 2 == 0:
            continue
        elif name in ("v", "wo"):
            ev += [(name, 4 * i + b, 4 * (i % 2) + b, "dve") for b in range(NB)]
        else:
            eng = {"cc": "act", "gc": "act", "ga": "act"}.get(name, "dve")
            ev += [(name, 2 * i + m, (t + m) % 4, eng) for m in range(2)]
            t += 2
    return ev


EVENTS = tile_events()
EV = {(kind, i): n for n, (kind, i, _, _) in enumerate(EVENTS)}
UNIT_OF = {}
for _u in range(UF):
    _name, _i = CHUNKS[_u // 2]
    if _name == "wba":
        UNIT_OF.update({(_name, 4 * (_u % 2) + m): _u for m in range(4)})
    elif _u % 2:
        _w = NB if _name in ("v", "wo") else 2
        UNIT_OF.update({(_name, _w * _i + m): _u for m in range(_w)})
FREED = []
for _kind, _i, _bank, _eng in EVENTS:
    FREED.append((_eng, 1 + sum(e == _eng for e, _ in FREED)))
DONE = {}
for _e in EVENTS:
    if _e[0] in ("xT", "ss"):
        DONE[_e[:2]] = len(DONE) + 1
BEFORE = []
for _n, _e in enumerate(EVENTS):
    BEFORE.append(max((m for m in range(_n) if EVENTS[m][2] == _e[2]), default=None))


def hybrid_block(nc, x, norm1_g, w_in, q_norm_g, k_norm_g, rel_bias, conv_w, w_branch_conv,
                 w_branch_attn, w_out, norm2_g, w_router, b_router, w_gate_up, b_gate_up, w_down,
                 b_down, consts, buckets, out):
    ctx = ExitStack()
    with ctx:
        def sb(name, shape, dt=F32):
            return ctx.enter_context(nc.sbuf_tensor(name, shape, dt))

        def sem(name):
            return ctx.enter_context(nc.semaphore(name))

        vec_dram = nc.dram_tensor("toeplitz_vectors", (NH, (NSH + 2) * VEC), F32, kind="Internal").ap()
        h2_dram = nc.dram_tensor("expert_inputs", (S, D), F32, kind="Internal").ap()
        y_dram = nc.dram_tensor("expert_outputs", (S * TOPK, D), F32, kind="Internal").ap()

        ps = ctx.enter_context(nc.psum_tensor("ps", [P, 8, 512], F32))

        raw = sb("raw", [P, RAW, CH])
        w_hi = sb("w_hi", [P, UN, UH], F32R)
        w_lo = sb("w_lo", [P, UN, UH], F32R)
        zT = sb("zT", [P, 2, KD, S], F32R)
        oT = sb("oT", [P, 2, 2, S], F32R)
        r1 = sb("r1", [P, 4 * D])
        r2 = sb("r2", [P, 6 * D])
        r3 = sb("r3", [P, 9 * 512])
        work = sb("work", [P, 4 * D])
        cst = sb("cst", [P, C_END])
        small = sb("small", [P, 34])
        stat = sb("stat", [P, 32])
        uix = sb("uix", [P, 4], U32)
        ublk = sb("ublk", [P, NCOL + 1], U32)

        with nc.sbuf_tensor("hT", [P, 2, KD, S], F32R) as hT:
            pass
        more_raw = sb("more_raw", [P, XRAW - RAW, CH])
        xT = sb("xT", [P, 2 * KD, P], F32R)

        ident = cst[:, C_ID:C_ID + P]
        ones = cst[:, C_ONE:C_ONE + P]
        xin = r1[:, :].rearrange("p (b d) -> p b d", b=NB)
        v_sb = r1[:, 0:NB * AW].rearrange("p (b d) -> p b d", b=NB)
        t1 = r1[:, :].rearrange("p (k s) -> p k s", k=KD)
        h2 = xin
        xs = r1[:, 0:D]
        ysb = r1[:, D:2 * D]
        bdn = r1[0:NE, 2 * D:3 * D]
        gT = r1[0:NE, 3 * D:3 * D + S]
        qk = r2[:, :].rearrange("p (j s) -> p j s", j=2 * QT)
        ya = r2[:, 0:4 * D].rearrange("p (k s) -> p k s", k=KD)
        x2 = r2[:, 0:4 * D].rearrange("p (b d) -> p b d", b=NB)
        bk_sb = r2[0:BUCKETS + 1, 0:(NSH + 2) * VEC]
        vec_sb = r2[0:NH, (NSH + 2) * VEC:2 * (NSH + 2) * VEC]
        g2b = r2[:, 4 * D:5 * D]
        tail = r2[:, 4 * D:6 * D]
        oh = tail[:, 0:512].rearrange("p (a e) -> p a e", e=NE)
        ohk = tail[:, 0:512].rearrange("p (b k e) -> p b k e", b=NB, k=TOPK)
        msk = tail[:, 512:640].rearrange("p (b e) -> p b e", b=NB)
        k4 = tail[:, 640:768].rearrange("p (b e) -> p b e", b=NB)
        gmat = tail[:, 768:896].rearrange("p (b e) -> p b e", b=NB)
        sg1 = tail[:, 896:1024].rearrange("p (b e) -> p b e", b=NB)
        lgt = tail[:, 1024:1152].rearrange("p (b e) -> p b e", b=NB)
        sg = tail[:, 1152:1152 + NB * NCOL].rearrange("p (b g) -> p b g", b=NB)
        lk = tail[:, 1344:1344 + NB * NCOL * 2].rearrange("p (b g c) -> p b g c", b=NB, c=2)
        top8 = tail[:, 1728:1760].rearrange("p (b k) -> p b k", b=NB)
        idxf = tail[:, 1760:1792].rearrange("p (b k) -> p b k", b=NB)
        idx8 = tail[:, 1792:1824].bitcast(U32).rearrange("p (b k) -> p b k", b=NB)
        gate = tail[:, 1824:1840].rearrange("p (b k) -> p b k", b=NB)
        eb = tail[:, 1840:1840 + NCOL]
        off32 = tail[:, 1888:1920]
        inc32 = tail[:, 1920:1952]
        nbk = tail[0:NE, 1952:1956]
        wr_sb = tail[:, 1152:1152 + KD * NE].rearrange("p (k e) -> p k e", k=KD)
        br_sb = tail[:, 1888:1920]
        tb1 = r3[:, 0:HPG * NSH * P].rearrange("p (h n) -> p h n", h=HPG)
        tb23 = r3[:, HPG * NSH * P:].rearrange("p (h g n) -> p h g n", h=HPG, g=2)
        bpart = r3[0:3 * NE, 0:D].bitcast(BF16)
        braw = r3[0:3 * NE, D:3 * D]
        btmp = r3[0:3 * NE, 3 * D:4 * D].bitcast(BF16)
        sel = r3[0:3 * NE, D:D + MAXBLK * P // 2].bitcast(BF16).rearrange("p (g n) -> p g n", n=P)
        cu = work[:, 0:1024].rearrange("p (m s) -> p m s", m=2)
        yv = work[:, 1024:2048].rearrange("p (m s) -> p m s", m=2)
        prob = work[:, 2048:2816]
        pT = work[:, 2816:3584]
        relm = work[0:BUCKETS + 1, 3584:3584 + NH]
        stage = work[0:34, 3600:3728]
        h2T = work[:, :].rearrange("p (k s) -> p k s", k=KD)
        act = work[:, 0:1024].rearrange("p (m n) -> p m n", m=2)
        g1b, u1b, sgb = work[:, 1024:1536], work[:, 1536:2048], work[:, 2048:2560]
        hot = work[:, 2560:3072].rearrange("p (b n) -> p b n", b=NB)
        ov1 = work[:, 3072:3072 + MAXOVER * NE].rearrange("p (j e) -> p j e", e=NE)
        ov2 = work[:, 3584:3584 + MAXOVER * NE].rearrange("p (j e) -> p j e", e=NE)
        xTh, xTl = xT[:, 0:KD], xT[:, KD:2 * KD]
        aT = oT[:, :, :, :].rearrange("p a b (c n) -> p (a b c) n", n=P)
        aTh, aTl = aT[:, 0:KD], aT[:, KD:2 * KD]
        ov3 = cu
        bk_A, bk_B, bk_D, bk_T = 0, 2, 4, 6

        x_in = [sem(f"x_in{b}") for b in range(NB)]
        c_in = sem("c_in")
        st_in = sem("st_in")
        bk_in = sem("bk_in")
        vec_out = sem("vec_out")
        tb_in = sem("tb_in")
        rawin = [sem(f"raw_in{r}") for r in range(RAW)]
        xraw_in = [sem(f"xraw_in{r}") for r in range(XRAW)]
        split_hi = sem("split_hi")
        split_lo = sem("split_lo")
        used = sem("used")
        relset = sem("relset")
        pe_small = sem("pe_small")
        small_rd = sem("small_rd")
        pe_vec = sem("pe_vec")
        vec_rd = sem("vec_rd")
        ssq = sem("ssq")
        eps_ok = sem("eps_ok")
        rstd_s = sem("rstd_s")
        xn_ok = sem("xn_ok")
        done = sem("done")
        freed = {"act": sem("freed_act"), "dve": sem("freed_dve")}
        hi_ok = sem("hi_ok")
        sq_ok = sem("sq_ok")
        at_s, at_l, at_nm, at_e, at_r, at_p = [
            sem(n) for n in ("at_s", "at_l", "at_nm", "at_e", "at_r", "at_p")]
        at_t, at_ta, at_td = [sem(n) for n in ("at_t", "at_ta", "at_td")]
        at_o, at_oh, at_ol = [sem(n) for n in ("at_o", "at_oh", "at_ol")]
        cc_ok, z_hi, z_lo = [sem(n) for n in ("cc_ok", "z_hi", "z_lo")]
        m_ok, m_hi, m_lo = [sem(n) for n in ("m_ok", "m_hi", "m_lo")]
        x2_in = sem("x2_in")
        g2_in = sem("g2_in")
        h2_ok = sem("h2_ok")
        h2_out = sem("h2_out")
        h2T_pe, h2T_ok = sem("h2T_pe"), sem("h2T_ok")
        wr_in = sem("wr_in")
        lgt_pe = sem("lgt_pe")
        gp_step = sem("gp_step")
        top_ok, ge_ok, m32_ok, rank_pe = [sem(n) for n in ("top_ok", "ge_ok", "m32_ok", "rank_pe")]
        nb_ok, off_pe, tab_ok, over_ok = [sem(n) for n in ("nb_ok", "off_pe", "tab_ok", "over_ok")]
        bd_in, gm_ok, gT_pe, gT_ok, bd_pe, x2b_ok = [
            sem(n) for n in ("bd_in", "gm_ok", "gT_pe", "gT_ok", "bd_pe", "x2b_ok")]
        b_in, bp_ok = sem("b_in"), sem("bp_ok")
        xs_set = sem("xs_set")
        chain = sem("chain")
        pchain = sem("pchain")
        col_ok = sem("col_ok")
        hot_ok = sem("hot_ok")
        t_pe = sem("t_pe")
        t_rd = sem("t_rd")
        t_hi = sem("t_hi")
        xs_in = sem("xs_in")
        g_ok, u_ok, tt_ok, sgm_ok, act_ok = [sem(n) for n in ("g_ok", "u_ok", "tt_ok", "sgm_ok", "act_ok")]
        y_ok, y_out = sem("y_ok"), sem("y_out")
        cp_ok = sem("cp_ok")
        rows_free = sem("rows_free")
        fin_in = [sem(f"fin_in{b}") for b in range(NB)]
        o_out = sem("o_out")

        T_BASE, H_BASE = 3, 2

        w_in_v = w_in[0].rearrange("(k p) n -> p k n", p=P)
        w_bc_v = w_branch_conv[0].rearrange("(k p) n -> p k n", p=P)
        w_ba_v = w_branch_attn[0].rearrange("(k p) n -> p k n", p=P)
        w_out_v = w_out[0].rearrange("(k p) n -> p k n", p=P)
        x_v = x[0].rearrange("(i b) d -> i b d", b=NB)
        out_v = out[0].rearrange("(i b) d -> i b d", b=NB)
        h2_v = h2_dram.rearrange("(i b) d -> i b d", b=NB)
        y_v = y_dram.rearrange("(i b k) d -> i b k d", b=NB, k=TOPK)

        def front_source(c):
            name, i = CHUNKS[c]
            cols = slice(256 * i, 256 * i + 256)
            if name == "wba":
                return w_ba_v
            if name == "wbc":
                return w_bc_v[:, :, cols]
            if name == "wo":
                return w_out_v[:, :, cols]
            return w_in_v[:, :, IN_COL[name] + 256 * i:IN_COL[name] + 256 * i + 256]

        def raw_unit(n, slot):
            half = raw[:, slot, UH * (n % 2):UH * (n % 2) + UH]
            if n < UF and CHUNKS[n // 2][0] == "wba":
                return raw[:, slot, :].rearrange("p (k n) -> p k n", k=2)[:, :, 512 * (n % 2):512 * (n % 2) + 512]
            return half

        def expert_raw(c):
            slot = (c + RAW) % XRAW
            return (raw[:, slot, :] if slot < RAW else more_raw[:, slot - RAW, :]), slot

        def expert_unit(i, j):
            slot = j % XUN
            if slot < UN:
                return (w_hi, w_lo)[i][:, slot, :]
            return zT[:, i, 2 * (slot - UN):2 * (slot - UN) + 2, :].rearrange("p k s -> p (k s)")

        def packed(t, n):
            if n < UF and CHUNKS[n // 2][0] == "wba":
                return t[:, n % UN, :].rearrange("p (k n) -> p k n", k=2)
            return t[:, n % UN, :]

        def toeplitz(head, g):
            v0 = 0 if g == 0 else NSH + g - 1
            nv = NSH if g == 0 else 1
            base = vec_dram[head:head + 1, VEC * v0:VEC * v0 + 1]
            return bass.AP(base.tensor, base.offset, [[1, P], [VEC, nv], [1, P]])

        block = ctx.enter_context(nc.Block())

        @block.sync
        def _(sp):
            sp.dma_start(cst[:, :], consts).then_inc(c_in, 16)
            for b in range(NB):
                sp.dma_start(xin[:, b, :], x_v[:, b, :]).then_inc(x_in[b], 16)
            sp.dma_start(stage[0:8, :], norm1_g[0].rearrange("(k p) -> k p", p=P)).then_inc(st_in, 16)
            sp.dma_start(stage[8:32, :], conv_w[0].rearrange("t (k p) -> (t k) p", p=P)).then_inc(st_in, 16)
            for half in range(2):
                sp.dma_start(stage[32:33, DH * half:DH * half + DH], q_norm_g).then_inc(st_in, 16)
                sp.dma_start(stage[33:34, DH * half:DH * half + DH], k_norm_g).then_inc(st_in, 16)
            sp.dma_start(bk_sb, buckets).then_inc(bk_in, 16)
            sp.dma_start(relm[0:BUCKETS, :], rel_bias).then_inc(bk_in, 16)

            def load_front(c):
                if c >= RAW:
                    sp.wait_ge(split_lo, 2 * (c - RAW) + 2)
                dst = raw[:, c % RAW, :].rearrange("p (k n) -> p k n", k=2 if CHUNKS[c][0] == "wba" else KD)
                sp.dma_start(dst, front_source(c)).then_inc(rawin[c % RAW], 16)

            for c in range(RAW):
                load_front(c)
            sp.wait_ge(vec_rd, 5)
            sp.dma_start(vec_dram, vec_sb).then_inc(vec_out, 16)
            sp.wait_ge(vec_out, 16)
            for h in range(HPG):
                sp.dma_start(tb1[:, h, :].rearrange("p (v n) -> p v n", n=P), toeplitz(h, 0)).then_inc(tb_in, 16)
                for g in (1, 2):
                    sp.dma_start(tb23[:, h, g - 1:g, :], toeplitz(HPG * g + h, g)).then_inc(tb_in, 16)
            for c in range(RAW, NF):
                load_front(c)
                if CHUNKS[c] == ("gc", 1):
                    sp.wait_ge(at_l, HPG * NB)
                    for part in range(3):
                        sp.dma_start(braw[NE * part:NE * part + NE, :], b_gate_up[0]).then_inc(b_in, 16)
                if CHUNKS[c] == ("wo", 3):
                    sp.wait_ge(m_ok, KD)
                    for b in range(NB):
                        sp.dma_start(x2[:, b, :], x_v[:, b, :]).then_inc(x2_in, 16)
                    sp.dma_start(g2b, bass.AP(
                        norm2_g.tensor, norm2_g.offset, [[0, P], [1, D]])).then_inc(g2_in, 16)

            def load_expert(c, e, nth):
                dst, slot = expert_raw(c)
                if nth is not None:
                    sp.wait_ge(split_lo, 2 * (nth - XRAW) + 2)
                if c < 8:
                    half, k0 = c // 4, 2 * (c % 4)
                    src = w_gate_up[0][bass.ds(e, 1)].rearrange("o (p k) (s n) -> p (o k s) n", p=P, s=2)[
                        :, 2 * k0:2 * k0 + 4, 512 * half:512 * half + 512]
                    dst = dst.rearrange("p (a n) -> p a n", a=4)
                else:
                    half, k0 = (c - 8) // 2, 2 * (c % 2)
                    src = w_down[0][bass.ds(e, 1)].rearrange("o (h p k) n -> p (o h) k n", h=2, p=P)[
                        :, half, k0:k0 + 2, :]
                    dst = dst.rearrange("p (k n) -> p k n", k=2)
                sp.dma_start(dst, src).then_inc(xraw_in[slot], 16)

            sp.wait_ge(used, 2 * CHUNKS.index(("wo", 0)))
            for c in range(RAW):
                load_expert(c, 0, None)
            sp.wait_ge(split_lo, UF)
            for c in range(RAW, XRAW):
                load_expert(c, 0, None)
            sp.wait_ge(h2_ok, NB)
            for b in range(NB):
                sp.dma_start(h2_v[:, b, :], h2[:, b, :]).then_inc(h2_out, 16)
            sp.dma_start(wr_sb, w_router[0].rearrange("(k p) e -> p k e", p=P)).then_inc(wr_in, 16)
            sp.dma_start(br_sb, bass.AP(b_router.tensor, b_router.offset, [[0, P], [1, NE]])).then_inc(wr_in, 16)
            sp.wait_ge(h2T_pe, KD)
            sp.wait_ge(h2_out, 16 * NB)
            sp.dma_start(bdn, b_down[0]).then_inc(bd_in, 16)
            for c in range(XRAW, CPE):
                load_expert(c, 0, NF + c)
            with sp.Fori(1, NE) as g:
                for c in range(CPE):
                    load_expert(c, g, CPE * g + (NF + c))
            sp.wait_ge(over_ok, 1)
            sp.wait_ge(tab_ok, 1)
            nblk = sp.value_load(ublk[0:1, NCOL:NCOL + 1], min_val=NE, max_val=MAXBLK)
            with sp.If(nblk > NE):
                with sp.Fori(NE, nblk) as g:
                    e = sp.value_load(ublk[0:1, bass.ds(g, 1)], min_val=0, max_val=NE - 1)
                    for c in range(CPE):
                        load_expert(c, e, CPE * g + (NF + c))
            sp.wait_ge(y_out, 16 * nblk)
            places = [raw[:, 0:2, :].rearrange("p a n -> p (a n)"),
                      more_raw[:, 0:2, :].rearrange("p a n -> p (a n)"), work[:, :], r3[:, 0:4 * D]]
            sp.wait_ge(used, UPE * nblk + UF)
            for b in range(NB):
                sp.dma_start(places[b].rearrange("p (k d) -> p k d", k=TOPK), y_v[:, b]).then_inc(fin_in[b], 16)
            for b in range(NB):
                sp.wait_ge(cp_ok, nblk + (TOPK * b + TOPK))
                sp.dma_start(out_v[:, b, :], x2[:, b, :]).then_inc(o_out, 16)
            sp.wait_ge(o_out, 16 * NB)

        @block.tensor
        def _(pe):
            def bank_free(ev):
                before = BEFORE[ev]
                if before is not None:
                    eng, n = FREED[before]
                    pe.wait_ge(freed[eng], n)

            def three(dst, a_hi, a_lo, b_hi, b_lo, start, stop):
                pe.matmul(dst, a_hi, b_hi, start=start, stop=False)
                pe.matmul(dst, a_hi, b_lo, start=False, stop=False)
                return pe.matmul(dst, a_lo, b_hi, start=False, stop=stop)

            pe.wait_ge(c_in, 16)
            pe.wait_ge(st_in, 16 * 6)
            pe.transpose(ps[:, 7, 0:34], stage, ident[0:34, 0:34]).then_inc(pe_small, 1)
            pe.wait_ge(bk_in, 32)
            pe.wait_ge(relset, 1)
            nv = (NSH + 2) * VEC
            for j in range(5):
                w = min(512, nv - 512 * j)
                pe.matmul(ps[0:NH, j, 0:w], relm, bk_sb[:, 512 * j:512 * j + w],
                          start=True, stop=True).then_inc(pe_vec, 1)
            pe.wait_ge(vec_rd, 5)
            pe.wait_ge(small_rd, 1)
            for b in range(NB):
                pe.wait_ge(xn_ok, b + 1)
            for k in range(KD):
                for b in range(NB):
                    last = pe.transpose(ps[:, k, P * b:P * b + P], xin[:, b, P * k:P * k + P], ident)
                last.then_inc(done, 1)

            def unit(n, tiles=(0, 1)):
                name, i = CHUNKS[n // 2]
                if 0 in tiles:
                    pe.wait_ge(split_lo, n + 1)
                wh, wl = w_hi[:, n % UN, :], w_lo[:, n % UN, :]
                h = n % 2
                if name == "wba":
                    wh = wh.rearrange("p (k n) -> p k n", k=2)
                    wl = wl.rearrange("p (k n) -> p k n", k=2)
                    pe.wait_ge(at_ol, HPG * NB)
                    for m in range(4):
                        ev = EV[("wba", 4 * h + m)]
                        bank_free(ev)
                        c = slice(P * m, P * m + P)
                        for k in range(2):
                            last = three(ps[:, EVENTS[ev][2], :], wh[:, k, c], wl[:, k, c],
                                         oT[:, 0, k, :], oT[:, 1, k, :], k == 0, k == 1)
                    return last
                wh = wh.rearrange("p (k n) -> p k n", k=4)
                wl = wl.rearrange("p (k n) -> p k n", k=4)
                if name in ("v", "wo"):
                    src = hT if name == "v" else zT
                    for b in range(NB):
                        ev = EV[(name, 4 * i + b)]
                        if h == 0:
                            bank_free(ev)
                        for k in range(4):
                            kk = 4 * h + k
                            if name == "wo" and b == 0:
                                pe.wait_ge(m_lo, kk + 1)
                            c = slice(P * b, P * b + P)
                            last = three(ps[:, EVENTS[ev][2], 0:256], src[:, 0, kk, c], src[:, 1, kk, c],
                                         wh[:, k, :], wl[:, k, :], kk == 0, kk == KD - 1)
                    return last
                src = zT if name == "wbc" else hT
                for m in tiles:
                    ev = EV[(name, 2 * i + m)]
                    if h == 0:
                        bank_free(ev)
                    for k in range(4):
                        kk = 4 * h + k
                        if m == 0:
                            pe.wait_ge(z_lo if name == "wbc" else freed["dve"], kk + 1)
                        c = slice(P * m, P * m + P)
                        last = three(ps[:, EVENTS[ev][2], :], wh[:, k, c], wl[:, k, c],
                                     src[:, 0, kk, :], src[:, 1, kk, :], kk == 0, kk == KD - 1)
                return last

            def square_sums(j):
                ev = EV[("ss", j)]
                bank_free(ev)
                pe.wait_ge(sq_ok, j + 1)
                pe.matmul(ps[:, EVENTS[ev][2], :], cst[:, C_BLK:C_BLK + P], yv[:, j % 2, :],
                          start=True, stop=True).then_inc(done, 1)

            def scores(u):
                hh, b = divmod(u, NB)
                half = slice(DH * (hh % 2), DH * (hh % 2) + DH)
                if u == 0:
                    pe.wait_ge(freed["dve"], FREED[EV[("k", QT - 1)]][1])
                    for bb in range(NB):
                        eng, n = FREED[EV[("v", NB + bb)]]
                        pe.wait_ge(freed[eng], n)
                else:
                    pe.wait_ge(at_l, u)
                for g in range(NG):
                    j = 2 * g + hh // 2
                    keys = slice(0, S) if g == 0 else slice(P * b, P * b + P)
                    dst = ps[:, 4, :] if g == 0 else ps[:, 5, P * (g - 1):P * g]
                    last = pe.matmul(dst, qk[half, j, P * b:P * b + P], qk[half, QT + j, keys],
                                     start=True, stop=True)
                last.then_inc(at_s, 1)

            def turn(u):
                pe.wait_ge(at_p, u + 1)
                if u:
                    pe.wait_ge(at_ol, u)
                for c in range(6):
                    last = pe.transpose(ps[:, 6 + c // 4, P * (c % 4):P * (c % 4) + P],
                                        prob[:, P * c:P * c + P], ident)
                last.then_inc(at_t, 1)

            def values(u):
                hh, b = divmod(u, NB)
                pe.wait_ge(at_ta, u + 1)
                pe.wait_ge(at_td, u + 1)
                dst = ps[DH * (hh % 2):DH * (hh % 2) + DH, 7, 256:256 + P]
                for c in range(6):
                    g = 0 if c < 4 else c - 3
                    head = HPG * g + hh
                    last = pe.matmul(dst, v_sb[:, c if c < 4 else b, DH * head:DH * head + DH],
                                     pT[:, P * c:P * c + P], start=(c == 0), stop=(c == 5))
                last.then_inc(at_o, 1)

            for kind, n in STEPS:
                if kind == "unit":
                    unit(n, (1,) if ("half", n) in STEPS else (0, 1)).then_inc(used, 1)
                elif kind == "half":
                    unit(n, (0,))
                elif kind == "ss":
                    square_sums(n)
                elif kind == "S":
                    scores(n)
                elif kind == "T":
                    turn(n)
                elif kind == "PV":
                    values(n)

            for k in range(KD):
                if k == 0:
                    pe.wait_ge(h2_ok, NB)
                for b in range(NB):
                    last = pe.transpose(ps[:, k, P * b:P * b + P], h2[:, b, P * k:P * k + P], ident)
                last.then_inc(h2T_pe, 1)
            pe.wait_ge(wr_in, 32)
            pe.wait_ge(h2T_ok, KD)
            for b in range(NB):
                for k in range(KD):
                    last = pe.matmul(ps[:, 0, NE * b:NE * b + NE], h2T[:, k, P * b:P * b + P], wr_sb[:, k, :],
                                     start=(k == 0), stop=(k == KD - 1))
            last.then_inc(lgt_pe, 1)
            pe.wait_ge(m32_ok, 1)
            for b in range(NB):
                for c in range(b + 1):
                    last = pe.matmul(ps[:, 1, NE * b:NE * b + NE], cst[:, C_TRI:C_TRI + P] if c == b else ones,
                                     msk[:, c, :], start=(c == 0), stop=(c == b))
            last.then_inc(rank_pe, 1)
            for b in range(NB):
                last = pe.matmul(ps[0:NE, 2, 0:1], msk[:, b, :], ones[:, 0:1], start=(b == 0), stop=(b == NB - 1))
            last.then_inc(rank_pe, 1)
            pe.wait_ge(nb_ok, 1)
            nb_all = nbk[:, 3:4].to_broadcast([NE, P])
            pe.matmul(ps[:, 3, 0:NE], nb_all, cst[0:NE, C_TRI:C_TRI + NE], start=True, stop=True)
            pe.matmul(ps[:, 3, NE:2 * NE], nb_all, cst[0:NE, C_TRI:C_TRI + NE], start=True, stop=False)
            pe.matmul(ps[:, 3, NE:2 * NE], nb_all, ident[0:NE, 0:NE], start=False, stop=True).then_inc(off_pe, 1)

            def lookup(g, nth):
                for b in range(NB):
                    last = pe.matmul(ps[:, bk_T, 0:2], hot[:, b, :], lk[:, b, bass.ds(g, 1), :],
                                     start=(b == 0), stop=(b == NB - 1))
                last.then_inc(t_pe, 1)

            def turn_rows(half):
                for k in range(4):
                    last = pe.transpose(ps[:, bk_T + half, P * k:P * k + P],
                                        xs[:, 4 * half + k::KD], ident)
                last.then_inc(t_pe, 1)

            def turn_act(half):
                for k in range(4):
                    last = pe.transpose(ps[:, bk_T + half, P * k:P * k + P], act[:, half, k::4], ident)
                last.then_inc(t_pe, 1)

            pe.wait_ge(tab_ok, 1)
            pe.wait_ge(hot_ok, NB)
            lookup(0, 0)
            pe.wait_ge(gm_ok, 1)
            for b in range(NB):
                last = pe.transpose(ps[0:NE, 0, P * b:P * b + P], gmat[:, b, :], ident)
            last.then_inc(gT_pe, 1)
            pe.wait_ge(xs_in, 16)
            turn_rows(0)
            turn_rows(1)
            pe.wait_ge(bp_ok, 1)
            pe.wait_ge(nb_ok, 2)
            nblk = pe.value_load(ublk[0:1, NCOL:NCOL + 1], min_val=NE, max_val=MAXBLK)
            with pe.Fori(0, nblk) as g:
                pe.wait_ge(t_rd, 5 * g + T_BASE)
                for j in range(UPE):
                    pe.wait_ge(split_lo, UPE * g + (UF + j + 1))
                    wh, wl = expert_unit(0, j), expert_unit(1, j)
                    if j < 16:
                        half, k = divmod(j, 8)
                        base = bk_A + 2 * half
                        if k == 0:
                            for s in range(2):
                                pe.matmul(ps[:, base + s, :], sel[:, bass.ds(g, 1), :],
                                          bpart[:, D * s + 512 * half:D * s + 512 * half + 512],
                                          start=True, stop=False)
                        for s in range(2):
                            c = slice(512 * s, 512 * s + 512)
                            last = three(ps[:, base + s, :], xTh[:, k, :], xTl[:, k, :], wh[:, c], wl[:, c],
                                         False, k == KD - 1)
                    else:
                        k = j - 16
                        if k == 0:
                            pe.wait_ge(y_ok, 2 * g + 2)
                            pe.wait_ge(t_rd, 5 * g + T_BASE + 2)
                        if k == 4:
                            pe.wait_ge(t_rd, 5 * g + T_BASE + 3)
                        for s in range(2):
                            c = slice(512 * s, 512 * s + 512)
                            last = three(ps[:, bk_D + s, :], aTh[:, k, :], aTl[:, k, :], wh[:, c], wl[:, c],
                                         k == 0, k == KD - 1)
                    last.then_inc(used, 1)
                    if j == 8:
                        pe.wait_ge(hot_ok, NB * g + 2 * NB)
                        lookup(g + 1, 0)
                    if j == 13:
                        pe.wait_ge(act_ok, 2 * g + 1)
                        pe.wait_ge(t_rd, 5 * g + T_BASE + 1)
                        turn_act(0)
                    if j == 18:
                        pe.wait_ge(act_ok, 2 * g + 2)
                        turn_act(1)
                    if j == 19:
                        pe.wait_ge(xs_in, 16 * g + 32)
                        turn_rows(0)
                    if j == 21:
                        turn_rows(1)

            pe.wait_ge(gT_ok, 1)
            pe.wait_ge(bd_in, 16)
            for b in range(NB):
                if b >= 2:
                    pe.wait_ge(x2b_ok, b - 1)
                for n in range(2):
                    last = pe.matmul(ps[:, 2 * (b % 2) + n, :], gT[:, P * b:P * b + P],
                                     bdn[:, 512 * n:512 * n + 512], start=True, stop=True)
                last.then_inc(bd_pe, 1)

        @block.scalar
        def _(sc):
            def split(n):
                sc.wait_ge(rawin[(n // 2) % RAW], 16 * (n // 2 // RAW + 1))
                if n >= UN:
                    sc.wait_ge(used, n - UN + 1)
                nc.scalar.activation(packed(w_hi, n), raw_unit(n, (n // 2) % RAW), ACT.Copy).then_inc(split_hi, 1)

            for b in range(NB):
                sc.wait_ge(x_in[b], 16)
                if b >= 2:
                    sc.wait_ge(ssq, b - 1)
                nc.scalar.activation(work[:, 0:D] if b % 2 == 0 else work[:, D:2 * D], xin[:, b, :], ACT.Square,
                                     accum_out=stat[:, b:b + 1]).then_inc(ssq, 1)
            sc.wait_ge(ssq, NB)
            sc.wait_ge(eps_ok, 1)
            nc.scalar.activation(stat[:, 4:8], stat[:, 0:4], ACT.Sqrt, scale=1.0 / D,
                                 bias=stat[:, 31:32]).then_inc(rstd_s, 1)
            for j in range(5):
                w = min(512, (NSH + 2) * VEC - 512 * j)
                sc.wait_ge(pe_vec, j + 1)
                nc.scalar.activation(vec_sb[:, 512 * j:512 * j + w], ps[0:NH, j, 0:w], ACT.Copy).then_inc(vec_rd, 1)
            for n in range(AHEAD):
                split(n)
            sc.wait_ge(small_rd, 1)
            for k in range(KD):
                sc.wait_ge(done, DONE[("xT", k)])
                nc.scalar.activation(hT[:, 0, k, :], ps[:, k, :], ACT.Copy, scale=small[:, k:k + 1]).then_inc(hi_ok, 1)

            for kind, n in STEPS:
                if kind == "unit":
                    if n + AHEAD < UF:
                        split(n + AHEAD)
                    name, i = CHUNKS[n // 2]
                    if name == "wba":
                        for m in range(4):
                            ev = EV[("wba", 4 * (n % 2) + m)]
                            sc.wait_ge(used, n + 1)
                            if n % 2 == 0 and m == 0:
                                sc.wait_ge(at_s, HPG * NB)
                            nc.scalar.activation(ya[:, 4 * (n % 2) + m, :], ps[:, EVENTS[ev][2], :],
                                                 ACT.Copy).then_inc(freed["act"], 1)
                    if n % 2 == 0:
                        continue
                    for m in range(2):
                        t = 2 * i + m
                        if name in ("q", "k"):
                            j = t + (QT if name == "k" else 0)
                            ev = EV[(name, t)]
                            sc.wait_ge(used, n + 1)
                            if j >= 2:
                                sc.wait_ge(done, DONE[("ss", j - 2)])
                            nc.scalar.activation(yv[:, j % 2, :], ps[:, EVENTS[ev][2], :],
                                                 ACT.Square).then_inc(sq_ok, 1)
                        if name == "cc":
                            ev = EV[(name, t)]
                            sc.wait_ge(used, n + 1)
                            if t == 0:
                                sc.wait_ge(freed["dve"], FREED[EV[("k", QT - 1)]][1])
                            if t >= 2:
                                sc.wait_ge(cc_ok, t - 1)
                            nc.scalar.activation(cu[:, m, :], ps[:, EVENTS[ev][2], :],
                                                 ACT.Copy).then_inc(freed["act"], 1)
                        if name == "cb":
                            sc.wait_ge(freed["dve"], FREED[EV[(name, t)]][1])
                            nc.scalar.activation(zT[:, 0, t, :], yv[:, m, :], ACT.Copy).then_inc(z_hi, 1)
                        if name in ("gc", "ga"):
                            ev = EV[(name, t)]
                            sc.wait_ge(used, n + 1)
                            if name == "gc" and t < 2:
                                sc.wait_ge(z_lo, KD)
                            elif name == "gc":
                                sc.wait_ge(freed["dve"], FREED[EV[("wbc", t - 2)]][1])
                            elif t < 2:
                                sc.wait_ge(freed["dve"], FREED[EV[("wbc", KD - 1)]][1])
                            else:
                                sc.wait_ge(m_lo, t - 1)
                            nc.scalar.activation(cu[:, m, :], ps[:, EVENTS[ev][2], :],
                                                 ACT.Sigmoid).then_inc(freed["act"], 1)
                        if name == "ga":
                            sc.wait_ge(m_ok, t + 1)
                            nc.scalar.activation(zT[:, 0, t, :], cu[:, m, :], ACT.Copy).then_inc(m_hi, 1)
                elif kind == "ss":
                    ev = EV[("ss", n)]
                    sc.wait_ge(done, DONE[("ss", n)])
                    if n >= 2:
                        j = n - 2
                        sc.wait_ge(freed["dve"], FREED[EV[("q", j) if j < QT else ("k", j - QT)]][1])
                    nc.scalar.activation(cu[:, n % 2, :], ps[:, EVENTS[ev][2], :], ACT.Sqrt,
                                         bias=stat[:, 31:32]).then_inc(freed["act"], 1)
                elif kind == "M":
                    sc.wait_ge(at_nm, n + 1)
                    nc.scalar.activation(prob, prob, ACT.Exp, bias=stat[:, 8:9],
                                         accum_out=stat[:, 9:10]).then_inc(at_e, 1)
                    sc.wait_ge(at_r, n + 1)
                    nc.scalar.activation(prob, prob, ACT.Copy, scale=stat[:, 11:12]).then_inc(at_p, 1)
                elif kind == "T":
                    sc.wait_ge(at_t, n + 1)
                    nc.scalar.activation(pT[:, 0:512], ps[:, 6, :], ACT.Copy).then_inc(at_ta, 1)
                elif kind == "PV":
                    hh, b = divmod(n, NB)
                    half = slice(DH * (hh % 2), DH * (hh % 2) + DH)
                    sc.wait_ge(at_o, n + 1)
                    nc.scalar.activation(oT[half, 0, hh // 2, P * b:P * b + P][:, ::-1], ps[half, 7, 256:256 + P],
                                         ACT.Copy).then_inc(at_oh, 1)

            for b in range(NB):
                sc.wait_ge(freed["dve"], FREED[EV[("wo", 4 * NB - 1)]][1])
                sc.wait_ge(m_lo, KD)
                sc.wait_ge(ssq, NB + b if b < 2 else NB + b - 1)
                nc.scalar.activation(work[:, D:2 * D] if b % 2 else work[:, 0:D], x2[:, b, :], ACT.Square,
                                     accum_out=stat[:, 12 + b:13 + b]).then_inc(ssq, 1)
            sc.wait_ge(ssq, 2 * NB)
            nc.scalar.activation(stat[:, 16:20], stat[:, 12:16], ACT.Sqrt, scale=1.0 / D,
                                 bias=stat[:, 31:32]).then_inc(rstd_s, 1)
            for k in range(0, KD, 2):
                sc.wait_ge(h2T_pe, k + 1)
                nc.scalar.activation(h2T[:, k, :], ps[:, k, :], ACT.Copy).then_inc(h2T_ok, 1)
            sc.wait_ge(top_ok, 1)
            nc.scalar.activation(gate, gate, ACT.Exp).then_inc(ge_ok, 1)
            for half in range(2):
                sc.wait_ge(t_pe, 2 + half)
                nc.scalar.activation(xTh[:, 4 * half:4 * half + 4, :],
                                     ps[:, bk_T + half, :].rearrange("p (k n) -> p k n", n=P),
                                     ACT.Copy).then_inc(t_hi, 1)
            sc.wait_ge(nb_ok, 2)
            sc.wait_ge(tab_ok, 1)
            nblk = sc.value_load(ublk[0:1, NCOL:NCOL + 1], min_val=NE, max_val=MAXBLK)

            def store_y(n):
                sc.wait_ge(used, UPE * n + UF)
                sc.wait_ge(rows_free, n + 1)
                for s in range(2):
                    nc.scalar.activation(ysb[:, 512 * s:512 * s + 512], ps[:, bk_D + s, :],
                                         ACT.Copy).then_inc(y_ok, 1)

            with sc.Fori(0, nblk) as g:
                def split_expert(j):
                    chunk, slot = expert_raw(j // 2)
                    sc.wait_ge(xraw_in[slot], 16 * (CPE // XRAW) * g + 16 * (j // 2 // XRAW + 1))
                    sc.wait_ge(used, UPE * g + (UF + j - XUN + 1))
                    nc.scalar.activation(expert_unit(0, j), chunk[:, UH * (j % 2):UH * (j % 2) + UH],
                                         ACT.Copy).then_inc(split_hi, 1)

                def turned(nth, dst, bank):
                    sc.wait_ge(t_pe, 5 * g + T_BASE + nth)
                    nc.scalar.activation(dst, ps[:, bank, :].rearrange("p (k n) -> p k n", n=P),
                                         ACT.Copy).then_inc(t_hi, 1)

                def sigmoid(half):
                    sc.wait_ge(g_ok, 2 * g + half + 1)
                    nc.scalar.activation(sgb, g1b, ACT.Sigmoid, scale=ALPHA).then_inc(sgm_ok, 1)

                for j in range(UPE):
                    split_expert(j)
                    if j == 5:
                        store_y(g)
                    if j == 10:
                        sigmoid(0)
                    if j == 16:
                        turned(2, aTh[:, 0:4, :], bk_T)
                    if j == 18:
                        sigmoid(1)
                    if j == 21:
                        turned(3, aTh[:, 4:8, :], bk_T + 1)
                        turned(4, xTh[:, 0:4, :], bk_T)
                turned(5, xTh[:, 4:8, :], bk_T + 1)
            store_y(nblk)

        @block.vector
        def _(ve):
            links = [0]

            def link(ins):
                links[0] += 1
                ins.then_inc(chain, 1)
                ve.wait_ge(chain, links[0])

            def split(n):
                ve.wait_ge(split_hi, n + 1)
                nc.vector.tensor_tensor(packed(w_lo, n), raw_unit(n, (n // 2) % RAW), packed(w_hi, n).bitcast(F32),
                                        ALU.subtract).then_inc(split_lo, 1)

            nc.vector.memset(stat[:, 31:32], EPS).then_inc(eps_ok, 1)
            nc.vector.memset(relm[BUCKETS:BUCKETS + 1, :], 1.0).then_inc(relset, 1)
            ve.wait_ge(pe_small, 1)
            link(nc.vector.tensor_copy(small[:, :], ps[:, 7, 0:34]))
            nc.vector.tensor_scalar(small[:, 32:33], small[:, 32:33], DH ** -0.5, None, ALU.mult).then_inc(small_rd, 1)
            ve.wait_ge(rstd_s, 1)
            link(nc.vector.reciprocal(stat[:, 4:8], stat[:, 4:8]))
            for b in range(NB):
                nc.vector.tensor_scalar(xin[:, b, :], xin[:, b, :], stat[:, 4 + b:5 + b], None,
                                        ALU.mult).then_inc(xn_ok, 1)
            for n in range(AHEAD):
                split(n)
            ve.wait_ge(small_rd, 1)
            for k in range(KD):
                ve.wait_ge(hi_ok, k + 1)
                nc.vector.scalar_tensor_tensor(hT[:, 1, k, :], ps[:, k, :], small[:, k:k + 1],
                                               hT[:, 0, k, :].bitcast(F32), ALU.mult,
                                               ALU.subtract).then_inc(freed["dve"], 1)

            def convolve(m, t):
                u, y = cu[:, m, :], yv[:, m, :]
                tap = [small[:, 8 + KD * i + t:9 + KD * i + t] for i in range(3)]
                link(nc.vector.tensor_scalar(y, u, tap[2], None, ALU.mult))

                def add(dst, src, w):
                    link(nc.vector.scalar_tensor_tensor(dst, src, w, dst, ALU.mult, ALU.add))

                add(y[:, P:S], u[:, 0:S - P], tap[1])
                add(y[:, 1:P], u[:, S - P:S - 1], tap[1])
                add(y[:, 2 * P:S], u[:, 0:S - 2 * P], tap[0])
                y2, u2 = [a.rearrange("p (b n) -> p b n", b=NB) for a in (y, u)]
                nc.vector.scalar_tensor_tensor(y2[:, 0:2, 1:P], u2[:, 2:4, 0:P - 1], tap[0], y2[:, 0:2, 1:P],
                                               ALU.mult, ALU.add).then_inc(cc_ok, 1)

            for kind, n in STEPS:
                if kind == "unit":
                    if n + AHEAD < UF:
                        split(n + AHEAD)
                    name, i = CHUNKS[n // 2]
                    if name == "cb" and n % 2 == 0:
                        convolve(1, 2 * i + 1)
                    if n % 2 == 0:
                        continue
                    if name in ("v", "wo"):
                        for b in range(NB):
                            ev = EV[(name, NB * i + b)]
                            ve.wait_ge(used, n + 1)
                            src = ps[:, EVENTS[ev][2], 0:256]
                            if name == "v":
                                nc.vector.tensor_copy(v_sb[:, b, 256 * i:256 * i + 256], src).then_inc(freed["dve"], 1)
                            else:
                                dst = x2[:, b, 256 * i:256 * i + 256]
                                if b == 0:
                                    ve.wait_ge(x2_in, 16 * NB)
                                    ve.wait_ge(m_lo, KD)
                                nc.vector.tensor_tensor(dst, src, dst, ALU.add).then_inc(freed["dve"], 1)
                        continue
                    for m in range(2):
                        t = 2 * i + m
                        if name == "cx":
                            ev = EV[(name, t)]
                            ve.wait_ge(freed["act"], FREED[EV[("cc", t)]][1])
                            ve.wait_ge(used, n + 1)
                            nc.vector.tensor_tensor(cu[:, m, :], cu[:, m, :], ps[:, EVENTS[ev][2], :],
                                                    ALU.mult).then_inc(freed["dve"], 1)
                        if name == "cx" and m == 1:
                            ve.wait_ge(freed["dve"], FREED[ev][1])
                            if t >= 2:
                                ve.wait_ge(z_hi, t - 1)
                            convolve(0, t - 1)
                        if name == "cb":
                            ev = EV[(name, t)]
                            ve.wait_ge(used, n + 1)
                            ve.wait_ge(cc_ok, t + 1)
                            nc.vector.tensor_tensor(yv[:, m, :], yv[:, m, :], ps[:, EVENTS[ev][2], :],
                                                    ALU.mult).then_inc(freed["dve"], 1)
                            ve.wait_ge(z_hi, t + 1)
                            nc.vector.tensor_tensor(zT[:, 1, t, :], yv[:, m, :], zT[:, 0, t, :].bitcast(F32),
                                                    ALU.subtract).then_inc(z_lo, 1)
                        if name == "wbc":
                            ev = EV[(name, t)]
                            ve.wait_ge(used, n + 1)
                            ve.wait_ge(freed["act"], FREED[EV[("gc", t)]][1])
                            if t == 0:
                                ve.wait_ge(at_o, HPG * NB)
                            nc.vector.tensor_tensor(t1[:, t, :], cu[:, m, :], ps[:, EVENTS[ev][2], :],
                                                    ALU.mult).then_inc(freed["dve"], 1)
                        if name == "ga":
                            ve.wait_ge(freed["act"], FREED[EV[("ga", t)]][1])
                            link(nc.vector.tensor_tensor(cu[:, m, :], cu[:, m, :], ya[:, t, :], ALU.mult))
                            nc.vector.tensor_tensor(cu[:, m, :], cu[:, m, :], t1[:, t, :], ALU.add).then_inc(m_ok, 1)
                            ve.wait_ge(m_hi, t + 1)
                            nc.vector.tensor_tensor(zT[:, 1, t, :], cu[:, m, :], zT[:, 0, t, :].bitcast(F32),
                                                    ALU.subtract).then_inc(m_lo, 1)
                elif kind == "ss":
                    j = n
                    proj = EV[("q", j) if j < QT else ("k", j - QT)]
                    ve.wait_ge(freed["act"], FREED[EV[("ss", j)]][1])
                    link(nc.vector.reciprocal(cu[:, j % 2, :], cu[:, j % 2, :]))
                    if j == 0:
                        ve.wait_ge(vec_out, 16)
                    g = small[:, 32:33] if j < QT else small[:, 33:34]
                    dst, a, b = [t.rearrange("p (b n) -> p b n", b=NB) for t in (
                        qk[:, j, :], ps[:, EVENTS[proj][2], :], cu[:, j % 2, :])]
                    if j < QT:
                        dst = dst[:, :, ::-1]
                    nc.vector.scalar_tensor_tensor(dst, a, g, b, ALU.mult, ALU.mult).then_inc(freed["dve"], 1)
                elif kind == "M":
                    hh, b = divmod(n, NB)
                    if n == 0:
                        ve.wait_ge(tb_in, 16 * NH)
                    else:
                        ve.wait_ge(at_t, n)
                    ve.wait_ge(at_s, n + 1)
                    lo = P * (NB - 1 - b)
                    nc.vector.tensor_tensor(prob[:, 0:512], ps[:, 4, :], tb1[:, hh, lo:lo + 512], ALU.add)
                    link(nc.vector.tensor_tensor(prob[:, 512:768], ps[:, 5, 0:256],
                                                 tb23[:, hh].rearrange("p g n -> p (g n)"), ALU.add))
                    nc.vector.tensor_reduce(stat[:, 10:11], prob, AX.X, ALU.max).then_inc(at_l, 1)
                    ve.wait_ge(at_l, n + 1)
                    nc.vector.tensor_scalar(stat[:, 8:9], stat[:, 10:11], -1.0, None, ALU.mult).then_inc(at_nm, 1)
                    ve.wait_ge(at_e, n + 1)
                    nc.vector.reciprocal(stat[:, 11:12], stat[:, 9:10]).then_inc(at_r, 1)
                elif kind == "T":
                    ve.wait_ge(at_t, n + 1)
                    nc.vector.tensor_copy(pT[:, 512:768], ps[:, 7, 0:256]).then_inc(at_td, 1)
                elif kind == "PV":
                    hh, b = divmod(n, NB)
                    half = slice(DH * (hh % 2), DH * (hh % 2) + DH)
                    ve.wait_ge(at_oh, n + 1)
                    hi, lo = [oT[half, i, hh // 2, P * b:P * b + P][:, ::-1] for i in range(2)]
                    nc.vector.tensor_tensor(lo, ps[half, 7, 256:256 + P], hi.bitcast(F32),
                                            ALU.subtract).then_inc(at_ol, 1)

            ve.wait_ge(rstd_s, 2)
            link(nc.vector.reciprocal(stat[:, 16:20], stat[:, 16:20]))
            ve.wait_ge(g2_in, 16)
            for b in range(NB):
                nc.vector.scalar_tensor_tensor(h2[:, b, :], x2[:, b, :], stat[:, 16 + b:17 + b], g2b,
                                               ALU.mult, ALU.mult).then_inc(h2_ok, 1)
            for k in range(1, KD, 2):
                ve.wait_ge(h2T_pe, k + 1)
                nc.vector.tensor_copy(h2T[:, k, :], ps[:, k, :]).then_inc(h2T_ok, 1)

            ve.wait_ge(lgt_pe, 1)
            link(nc.vector.tensor_tensor(lgt, ps[:, 0, 0:P].rearrange("p (b e) -> p b e", b=NB),
                                         br_sb.unsqueeze(1).to_broadcast([P, NB, NE]), ALU.add))
            for b in range(NB):
                link(nc.vector.max(top8[:, b, :], lgt[:, b, :]))
                link(nc.vector.max_index(idx8[:, b, :], top8[:, b, :], lgt[:, b, :]))
            link(nc.vector.tensor_scalar(idxf[:, :, 0:TOPK], idx8[:, :, 0:TOPK], 1.0, None, ALU.add))
            for b in range(NB):
                nc.vector.tensor_tensor(ohk[:, b], idxf[:, b, 0:TOPK].unsqueeze(2).to_broadcast([P, TOPK, NE]),
                                        cst[:, C_IOTA:C_IOTA + NE].unsqueeze(1).to_broadcast([P, TOPK, NE]),
                                        ALU.is_equal)
            nc.vector.tensor_tensor(gate, top8[:, :, 0:TOPK], top8[:, :, 0:1].to_broadcast([P, NB, TOPK]),
                                    ALU.subtract).then_inc(top_ok, 1)
            ve.wait_ge(top_ok, 1)
            nc.vector.tensor_reduce(msk, ohk.rearrange("p b k e -> p b e k"), AX.X, ALU.add).then_inc(m32_ok, 1)
            link(nc.vector.scalar_tensor_tensor(k4, ohk[:, :, 2, :], 2.0, ohk[:, :, 1, :], ALU.mult, ALU.add))
            link(nc.vector.scalar_tensor_tensor(k4, ohk[:, :, 3, :], 3.0, k4, ALU.mult, ALU.add))
            for b in range(NB):
                nc.vector.tensor_scalar(lk[:, b, 0:NE, 1], k4[:, b, :], cst[:, C_TOK4 + b:C_TOK4 + b + 1], None,
                                        ALU.add)
                last = nc.vector.tensor_scalar(lk[:, b, :, 0], cst[:, C_ONE:C_ONE + NCOL],
                                               cst[:, C_TOK + b:C_TOK + b + 1], None, ALU.mult)
            link(last)
            ve.wait_ge(rank_pe, 1)
            ve.wait_ge(m32_ok, 1)
            link(nc.vector.scalar_tensor_tensor(sg1, ps[:, 1, 0:P].rearrange("p (b e) -> p b e", b=NB), 1.0, msk,
                                                ALU.add, ALU.mult))
            nc.vector.tensor_copy(sg[:, :, 0:NE], sg1).then_inc(tab_ok, 1)
            ve.wait_ge(rank_pe, 2)
            link(nc.vector.tensor_scalar(nbk[:, 0:1], ps[0:NE, 2, 0:1], P + 0.5, None, ALU.is_gt))
            link(nc.vector.tensor_scalar(nbk[:, 1:2], ps[0:NE, 2, 0:1], 2 * P + 0.5, None, ALU.is_gt))
            link(nc.vector.tensor_scalar(nbk[:, 2:3], ps[0:NE, 2, 0:1], 3 * P + 0.5, None, ALU.is_gt))
            link(nc.vector.tensor_tensor(nbk[:, 0:1], nbk[:, 0:1], nbk[:, 1:2], ALU.add))
            nc.vector.tensor_tensor(nbk[:, 3:4], nbk[:, 0:1], nbk[:, 2:3], ALU.add).then_inc(nb_ok, 1)

            def row_numbers(g):
                ve.wait_ge(t_pe, 5 * g + T_BASE + 1)
                nc.vector.tensor_scalar(uix[:, 0:2], ps[:, bk_T, 0:2], float(OUT_OF_RANGE), None,
                                        ALU.add).then_inc(t_rd, 1)

            ve.wait_ge(t_pe, 1)
            nc.vector.tensor_scalar(uix[:, 0:2], ps[:, bk_T, 0:2], float(OUT_OF_RANGE), None,
                                    ALU.add).then_inc(t_rd, 1)
            ve.wait_ge(off_pe, 1)
            nc.vector.tensor_copy(off32, ps[:, 3, 0:NE])
            link(nc.vector.tensor_copy(inc32, ps[:, 3, NE:2 * NE]))
            nc.vector.tensor_scalar(ublk[:, NCOL:NCOL + 1], ps[:, 3, 2 * NE - 1:2 * NE], float(NE), None,
                                    ALU.add).then_inc(nb_ok, 1)
            ve.wait_ge(ge_ok, 1)
            link(nc.vector.tensor_reduce(stat[:, 20:24], gate, AX.X, ALU.add))
            link(nc.vector.reciprocal(stat[:, 20:24], stat[:, 20:24]))
            link(nc.vector.tensor_tensor(gate, gate, stat[:, 20:24].unsqueeze(2).to_broadcast([P, NB, TOPK]),
                                         ALU.mult))
            for b in range(NB):
                last = nc.vector.tensor_tensor(ohk[:, b], ohk[:, b],
                                               gate[:, b, :].unsqueeze(2).to_broadcast([P, TOPK, NE]), ALU.mult)
            link(last)
            nc.vector.tensor_reduce(gmat, ohk.rearrange("p b k e -> p b e k"), AX.X, ALU.add).then_inc(gm_ok, 1)
            ve.wait_ge(gT_pe, 1)
            ve.wait_ge(h2_out, 16 * NB)
            nc.vector.tensor_copy(gT, ps[0:NE, 0, :]).then_inc(gT_ok, 1)
            for half in range(2):
                ve.wait_ge(t_hi, half + 1)
                dst = xTl[:, 4 * half:4 * half + 4, :]
                nc.vector.tensor_tensor(dst, ps[:, bk_T + half, :].rearrange("p (k n) -> p k n", n=P),
                                        xTh[:, 4 * half:4 * half + 4, :].bitcast(F32),
                                        ALU.subtract).then_inc(t_rd, 1)
            nblk = ve.value_load(ublk[0:1, NCOL:NCOL + 1], min_val=NE, max_val=MAXBLK)
            with ve.Fori(0, nblk) as g:
                def split_expert(j):
                    chunk, _ = expert_raw(j // 2)
                    ve.wait_ge(split_hi, UPE * g + (UF + j + 1))
                    nc.vector.tensor_tensor(expert_unit(1, j), chunk[:, UH * (j % 2):UH * (j % 2) + UH],
                                            expert_unit(0, j).bitcast(F32), ALU.subtract).then_inc(split_lo, 1)

                def activate(half):
                    bank = bk_A + 2 * half
                    ve.wait_ge(used, UPE * g + (UF + 8 * half + 8))
                    nc.vector.tensor_scalar(g1b, ps[:, bank, :], LIMIT, None, ALU.min).then_inc(g_ok, 1)
                    nc.vector.tensor_scalar(u1b, ps[:, bank + 1, :], LIMIT, -LIMIT, ALU.min,
                                            ALU.max).then_inc(u_ok, 1)
                    ve.wait_ge(u_ok, 2 * g + (half + 1))
                    nc.vector.scalar_tensor_tensor(u1b, u1b, 1.0, g1b, ALU.add, ALU.mult).then_inc(tt_ok, 1)
                    ve.wait_ge(tt_ok, 2 * g + (half + 1))
                    ve.wait_ge(sgm_ok, 2 * g + (half + 1))
                    nc.vector.tensor_tensor(act[:, half, :], u1b, sgb, ALU.mult).then_inc(act_ok, 1)

                def turned(nth, hi, lo, bank):
                    ve.wait_ge(t_hi, 4 * g + H_BASE + nth)
                    nc.vector.tensor_tensor(lo, ps[:, bank, :].rearrange("p (k n) -> p k n", n=P), hi.bitcast(F32),
                                            ALU.subtract).then_inc(t_rd, 1)

                for j in range(UPE):
                    split_expert(j)
                    if j == 10:
                        activate(0)
                    if j == 12:
                        ve.wait_ge(rows_free, g + 2)
                        nc.vector.tensor_copy(uix[:, 2:3], uix[:, 1:2]).then_inc(cp_ok, 1)
                        ve.wait_ge(cp_ok, g + 1)
                        row_numbers(g)
                    if j == 16:
                        turned(1, aTh[:, 0:4, :], aTl[:, 0:4, :], bk_T)
                    if j == 18:
                        activate(1)
                    if j == 21:
                        turned(2, aTh[:, 4:8, :], aTl[:, 4:8, :], bk_T + 1)
                        turned(3, xTh[:, 0:4, :], xTl[:, 0:4, :], bk_T)
                turned(4, xTh[:, 4:8, :], xTl[:, 4:8, :], bk_T + 1)

            for b in range(NB):
                ve.wait_ge(bd_pe, b + 1)
                nc.vector.tensor_tensor(x2[:, b, :], x2[:, b, :],
                                        ps[:, 2 * (b % 2):2 * (b % 2) + 2, :].rearrange("p a n -> p (a n)"),
                                        ALU.add).then_inc(x2b_ok, 1)
            ve.wait_ge(x2b_ok, NB)
            places = [raw[:, 0:2, :].rearrange("p a n -> p (a n)"),
                      more_raw[:, 0:2, :].rearrange("p a n -> p (a n)"), work[:, :], r3[:, 0:4 * D]]
            for b in range(NB):
                ve.wait_ge(fin_in[b], 16)
                for k in range(TOPK):
                    nc.vector.scalar_tensor_tensor(x2[:, b, :], places[b][:, D * k:D * k + D], gate[:, b, k:k + 1],
                                                   x2[:, b, :], ALU.mult, ALU.add).then_inc(cp_ok, 1)
                    if k + 1 < TOPK:
                        ve.wait_ge(cp_ok, nblk + (TOPK * b + k + 1))

        @block.gpsimd
        def _(gp):
            links = [0]

            def link(ins):
                links[0] += 1
                ins.then_inc(pchain, 1)
                gp.wait_ge(pchain, links[0])

            gp.sem_inc(rows_free, 2)
            gp.wait_ge(b_in, 16 * 3)
            gp.wait_ge(c_in, 16)
            link(nc.gpsimd.tensor_copy(bpart, braw))
            link(nc.gpsimd.tensor_tensor(braw, braw, bpart, ALU.subtract))
            link(nc.gpsimd.tensor_copy(btmp, braw))
            link(nc.gpsimd.tensor_copy(bpart[NE:2 * NE, :], btmp[NE:2 * NE, :]))
            link(nc.gpsimd.tensor_tensor(braw, braw, btmp, ALU.subtract))
            nc.gpsimd.tensor_copy(bpart[2 * NE:3 * NE, :], braw[2 * NE:3 * NE, :]).then_inc(bp_ok, 1)
            gp.wait_ge(bp_ok, 1)
            link(nc.gpsimd.tensor_scalar(
                sel[:, 0:NE, :], cst[0:3 * NE, C_IOTA:C_IOTA + NE].unsqueeze(2).to_broadcast([3 * NE, NE, P]),
                cst[0:3 * NE, C_RMOD:C_RMOD + 1], None, ALU.is_equal))
            gp.wait_ge(h2_out, 16 * NB)
            gp.wait_ge(h2T_pe, KD)
            nc.gpsimd.memset(xs, 0.0).then_inc(xs_set, 1)

            last_token, last_row = gp.to_reg(S - 1), gp.to_reg(S * TOPK - 1)

            def slots(g):
                nc.gpsimd.tensor_copy(stat[:, 24:28], sg[:, :, bass.ds(g, 1)].rearrange("p b o -> p (b o)")
                                      ).then_inc(col_ok, 1)
                gp.wait_ge(col_ok, g + 1)
                gp.sem_inc(gp_step, 1)
                for b in range(NB):
                    nc.gpsimd.tensor_scalar(hot[:, b, :], cst[:, C_IOTA:C_IOTA + P], stat[:, 24 + b:25 + b], None,
                                            ALU.is_equal).then_inc(hot_ok, 1)

            def gather():
                nc.gpsimd.indirect_dma_start(
                    out=xs, out_offset=None, in_=h2_dram,
                    in_offset=bass.IndirectOffsetOnAxis(ap=uix[:, 0:1], axis=0),
                    bounds_check=last_token, oob_is_err=False).then_inc(xs_in, 16)

            gp.wait_ge(tab_ok, 1)
            gp.wait_ge(lgt_pe, 1)
            slots(0)
            gp.wait_ge(xs_set, 1)
            gp.wait_ge(t_rd, 1)
            gather()

            jrow = cst[:, C_IOTA:C_IOTA + MAXOVER].unsqueeze(2).to_broadcast([P, MAXOVER, NE])
            erow = cst[:, C_IOTA:C_IOTA + NE].unsqueeze(1).to_broadcast([P, MAXOVER, NE])
            off_b = off32.unsqueeze(1).to_broadcast([P, MAXOVER, NE])
            inc_b = inc32.unsqueeze(1).to_broadcast([P, MAXOVER, NE])
            over = slice(NE, MAXBLK)

            def total(dst, src):
                w = NE
                while w > 2:
                    w //= 2
                    link(nc.gpsimd.tensor_tensor(src[:, :, 0:w], src[:, :, 0:w], src[:, :, w:2 * w], ALU.add))
                link(nc.gpsimd.tensor_tensor(dst, src[:, :, 0], src[:, :, 1], ALU.add))

            def over_experts():
                link(nc.gpsimd.tensor_tensor(ov1, jrow, off_b, ALU.subtract))
                link(nc.gpsimd.tensor_scalar(ov1, ov1, 0.5, None, ALU.is_gt))
                link(nc.gpsimd.tensor_tensor(ov2, jrow, inc_b, ALU.subtract))
                link(nc.gpsimd.tensor_scalar(ov2, ov2, 0.5, None, ALU.is_lt))
                link(nc.gpsimd.tensor_tensor(ov1, ov1, ov2, ALU.mult))
                link(nc.gpsimd.tensor_tensor(ov2, ov1, erow, ALU.mult))
                link(nc.gpsimd.tensor_copy(eb[:, 0:NE], cst[:, C_IOTA:C_IOTA + NE]))
                link(nc.gpsimd.memset(eb[:, MAXBLK:NCOL], 1.0))
                link(nc.gpsimd.memset(sg[:, :, MAXBLK:NCOL], 0.0))
                link(nc.gpsimd.memset(lk[:, :, MAXBLK:NCOL, 1], 0.0))
                total(eb[:, over], ov2)

            def over_slots(b):
                link(nc.gpsimd.tensor_tensor(ov2, off_b, jrow, ALU.subtract))
                link(nc.gpsimd.tensor_scalar(ov2, ov2, float(P), None, ALU.mult))
                link(nc.gpsimd.tensor_tensor(ov2, ov2, sg1[:, b, :].unsqueeze(1).to_broadcast([P, MAXOVER, NE]),
                                             ALU.add))
                link(nc.gpsimd.tensor_tensor(ov2, ov2, ov1, ALU.mult))
                total(sg[:, b, over], ov2)
                link(nc.gpsimd.tensor_tensor(ov2, ov1, k4[:, b, :].unsqueeze(1).to_broadcast([P, MAXOVER, NE]),
                                             ALU.mult))
                total(lk[:, b, over, 1], ov2)
                link(nc.gpsimd.tensor_scalar(lk[:, b, over, 1], lk[:, b, over, 1],
                                             cst[:, C_TOK4 + b:C_TOK4 + b + 1], None, ALU.add))

            def over_selectors():
                link(nc.gpsimd.tensor_scalar(sel[:, over, :], eb[0:3 * NE, over].unsqueeze(2).to_broadcast(
                    [3 * NE, MAXOVER, P]), cst[0:3 * NE, C_RMOD:C_RMOD + 1], None, ALU.is_equal))
                link(nc.gpsimd.tensor_scalar(eb, eb, 1.0, -1.0, ALU.max, ALU.add))
                nc.gpsimd.tensor_copy(ublk[:, 0:NCOL], eb).then_inc(over_ok, 1)
                gp.wait_ge(over_ok, 1)

            gp.wait_ge(nb_ok, 2)
            nblk = gp.value_load(ublk[0:1, NCOL:NCOL + 1], min_val=NE, max_val=MAXBLK)

            def gather_next(g):
                gp.wait_ge(t_pe, 5 * g + T_BASE)
                slots(g + 1)
                gp.wait_ge(t_rd, 5 * g + T_BASE + 1)
                gp.sem_inc(gp_step, 1)
                gather()

            def scatter(g):
                gp.wait_ge(y_ok, 2 * g + 4)
                gp.wait_ge(cp_ok, g + 1)
                gp.sem_inc(gp_step, 1)
                nc.gpsimd.indirect_dma_start(
                    out=y_dram, out_offset=bass.IndirectOffsetOnAxis(ap=uix[:, 2:3], axis=0),
                    in_=ysb, in_offset=None, bounds_check=last_row, oob_is_err=False).then_inc(y_out, 16)
                gp.wait_ge(y_out, 16 * g + 16)
                gp.sem_inc(rows_free, 1)

            for g in range(NB + 2):
                gather_next(g)
                if g == 0:
                    over_experts()
                elif g <= NB:
                    over_slots(g - 1)
                else:
                    over_selectors()
                scatter(g)
            with gp.Fori(NB + 2, nblk) as g:
                gather_next(g)
                scatter(g)


INS = ["x", "norm1_g", "w_in", "q_norm_g", "k_norm_g", "rel_bias", "conv_w", "w_branch_conv", "w_branch_attn",
       "w_out", "norm2_g", "w_router", "b_router", "w_gate_up", "b_gate_up", "w_down", "b_down"]


def kernel(**inputs):
    import concourse.bacc as bacc
    from concourse.bass_utils import run_bass_kernel_spmd

    nc = bacc.Bacc("TRN2", target_bir_lowering=False, num_devices=1)
    arrays, args = {}, []
    given = {name: np.ascontiguousarray(inputs[name]) for name in INS}
    given["consts"] = constants()
    given["buckets"] = bucket_rows()
    for name, a in given.items():
        arrays[f"in_{name}"] = a
        args.append(nc.dram_tensor(f"in_{name}", a.shape, mybir.dt.from_np(a.dtype), kind="ExternalInput").ap())
    args.append(nc.dram_tensor("out", (1, S, D), F32, kind="ExternalOutput").ap())
    hybrid_block(nc, *args)
    r = run_bass_kernel_spmd(nc, [arrays], core_ids=[0])
    return r.results[0]["out"]
```

```python
import math
from contextlib import ExitStack

import numpy as np

import concourse.bass as bass
from concourse import mybir

F32 = mybir.dt.float32
F32R = mybir.dt.float32r
BF16 = mybir.dt.bfloat16
U32 = mybir.dt.uint32
ALU = mybir.AluOpType
ACT = mybir.ActivationFunctionType
AX = mybir.AxisListType

P = 128
D = 1024
S = 512
NB = S // P
KD = D // P
DH = 64
HPG = 4
NG = 3
NH = HPG * NG
QT = NH * DH // P
AW = NH * DH
NE = 32
TOPK = 4
LIMIT = 7.0
ALPHA = 1.702
EPS = 1e-6
BUCKETS = 32
WINDOWS = ((128, 1), (512, 4), (2048, 16))
MAXDIST = 2048
NEG = -1e30
NSH = 2 * NB - 1
VEC = 2 * P

MAXOVER = S * TOPK // (P + 1)
MAXBLK = NE + MAXOVER
NCOL = MAXBLK + 1
OUT_OF_RANGE = 1 << 14

RAW = 3
UN = 4
XRAW, XUN = 6, 8
CH = 2048
UH = CH // 2
AHEAD = 3

C_ID, C_TRI, C_BLK, C_ONE, C_IOTA = 0, 128, 256, 384, 512
C_TOK, C_TOK4, C_RMOD = 640, 644, 648
C_END = 649


def constants():
    c = np.zeros((P, C_END), np.float32)
    p = np.arange(P)
    c[:, C_ID:C_ID + P] = np.eye(P)
    c[:, C_TRI:C_TRI + P] = p[:, None] < p[None, :]
    c[:, C_BLK:C_BLK + P] = (p[:, None] // DH == p[None, :] // DH) / DH
    c[:, C_ONE:C_ONE + P] = 1.0
    c[:, C_IOTA:C_IOTA + P] = p[None, :] + 1
    for b in range(NB):
        c[:, C_TOK + b] = NB * p + b - OUT_OF_RANGE
        c[:, C_TOK4 + b] = TOPK * (NB * p + b) - OUT_OF_RANGE
    c[:, C_RMOD] = p % NE + 1
    return c


def bucket(dist):
    exact = BUCKETS // 2
    d = np.maximum(dist.astype(np.float32), np.float32(1.0))
    large = exact + (np.log(d / np.float32(exact)) / np.float32(math.log(MAXDIST / exact))
                     * np.float32(BUCKETS - exact)).astype(np.int32)
    return np.where(dist < exact, dist, np.minimum(large, BUCKETS - 1))


def bucket_rows():
    n = np.arange(VEC) - (P - 1)
    rows = np.zeros((BUCKETS + 1, NSH + 2, VEC), np.float32)
    for v in range(NSH + 2):
        g = max(0, v - NSH + 1)
        window, dil = WINDOWS[g]
        dist = -NB * n + (NB - 1 - v if g == 0 else 0)
        ok = (dist >= 0) & (dist <= window) & (dist % dil == 0)
        rows[bucket(np.maximum(dist, 0)), v, np.arange(VEC)] = ok
        rows[BUCKETS, v] = np.where(ok, 0.0, NEG)
    return rows.reshape(BUCKETS + 1, -1)


def weight_chunks():
    order = [("q", i) for i in range(3)] + [("k", i) for i in range(3)] + [("v", i) for i in range(3)]
    for i in range(4):
        order += [("cc", i), ("cx", i), ("cb", i)]
    order += [("gc", 0), ("wba", 0), ("wbc", 0)]
    for i in range(1, 4):
        order += [("gc", i), ("wbc", i)]
    order += [("ga", i) for i in range(4)]
    order += [("wo", i) for i in range(4)]
    return order


CHUNKS = weight_chunks()
NF = len(CHUNKS)
UF = 2 * NF
CPE = 12
UPE = 2 * CPE
IN_COL = {"cb": 0, "cc": D, "cx": 2 * D, "q": 3 * D, "k": 3 * D + AW, "v": 3 * D + 2 * AW,
          "gc": 3 * D + 3 * AW, "ga": 4 * D + 3 * AW}


def front_steps():
    steps, unit = [], 0

    def units(n):
        nonlocal unit
        for _ in range(n):
            steps.append(("unit", unit))
            unit += 1

    for c in range(6):
        units(1)
        if c:
            steps.extend([("ss", 2 * c - 2), ("ss", 2 * c - 1)])
        units(1)
    units(1)
    steps.extend([("ss", 10), ("ss", 11)])
    units(5)
    halves = [(kind, n) for n in range(unit, unit + 24) for kind in ("half", "unit")]
    unit += 24
    steps.extend([halves[0], ("S", 0), ("M", 0)])
    for u in range(HPG * NB):
        steps.extend(halves[3 * u + (u == 0):3 * u + 2])
        if u + 1 < HPG * NB:
            steps.append(("S", u + 1))
        steps.append(("T", u))
        if u + 1 < HPG * NB:
            steps.append(("M", u + 1))
        steps.append(halves[3 * u + 2])
        steps.append(("PV", u))
    units(UF - unit)
    return steps


STEPS = front_steps()


def tile_events():
    ev = [("xT", k, k, "dve") for k in range(KD)]
    t = 0
    for kind, n in STEPS:
        if kind == "ss":
            ev.append(("ss", n, 4 + n % 4 if n < 10 else n % 2, "act"))
        if kind != "unit":
            continue
        name, i = CHUNKS[n // 2]
        if name == "wba":
            ev += [("wba", 4 * (n % 2) + m, 4 * (n % 2) + m, "act") for m in range(4)]
        elif n % 2 == 0:
            continue
        elif name in ("v", "wo"):
            ev += [(name, 4 * i + b, 4 * ((i + 1) % 2) + b, "dve") for b in range(NB)]
        else:
            eng = {"cc": "act", "gc": "act", "ga": "act"}.get(name, "dve")
            ev += [(name, 2 * i + m, (t + m) % 4, eng) for m in range(2)]
            t += 2
    return ev


EVENTS = tile_events()
EV = {(kind, i): n for n, (kind, i, _, _) in enumerate(EVENTS)}
FREED = []
for _kind, _i, _bank, _eng in EVENTS:
    FREED.append((_eng, 1 + sum(e == _eng for e, _ in FREED)))
DONE = {}
for _e in EVENTS:
    if _e[0] in ("xT", "ss"):
        DONE[_e[:2]] = len(DONE) + 1
BEFORE = []
for _n, _e in enumerate(EVENTS):
    BEFORE.append(max((m for m in range(_n) if EVENTS[m][2] == _e[2]), default=None))


def hybrid_block(nc, x, norm1_g, w_in, q_norm_g, k_norm_g, rel_bias, conv_w, w_branch_conv,
                 w_branch_attn, w_out, norm2_g, w_router, b_router, w_gate_up, b_gate_up, w_down,
                 b_down, consts, buckets, out):
    ctx = ExitStack()
    with ctx:
        def sb(name, shape, dt=F32):
            return ctx.enter_context(nc.sbuf_tensor(name, shape, dt))

        def sem(name):
            return ctx.enter_context(nc.semaphore(name))

        vec_dram = nc.dram_tensor("toeplitz_vectors", (NH, (NSH + 2) * VEC), F32, kind="Internal").ap()
        h2_dram = nc.dram_tensor("expert_inputs", (S, D), F32, kind="Internal").ap()
        y_dram = nc.dram_tensor("expert_outputs", (S * TOPK, D), F32, kind="Internal").ap()

        ps = ctx.enter_context(nc.psum_tensor("ps", [P, 8, 512], F32))

        raw = sb("raw", [P, RAW, CH])
        w_hi = sb("w_hi", [P, UN, UH], F32R)
        w_lo = sb("w_lo", [P, UN, UH], F32R)
        zT = sb("zT", [P, 2, KD, S], F32R)
        oT = sb("oT", [P, 2, 2, S], F32R)
        r1 = sb("r1", [P, 4 * D])
        r2 = sb("r2", [P, 6 * D])
        r3 = sb("r3", [P, 9 * 512])
        work = sb("work", [P, 4 * D])
        cst = sb("cst", [P, C_END])
        small = sb("small", [P, 34 + KD])
        stat = sb("stat", [P, 32 + 4 * NB])
        uix = sb("uix", [P, 5], U32)
        ushift = sb("ushift", [P, 3], U32)
        ublk = sb("ublk", [P, NCOL + 2], U32)

        with nc.sbuf_tensor("hT", [P, 2, KD, S], F32R) as hT:
            pass
        more_raw = sb("more_raw", [P, XRAW - RAW, CH])
        xT = sb("xT", [P, 2 * KD, P], F32R)

        ident = cst[:, C_ID:C_ID + P]
        ones = cst[:, C_ONE:C_ONE + P]
        xin = r1[:, :].rearrange("p (b d) -> p b d", b=NB)
        v_sb = r1[:, 0:NB * AW].rearrange("p (b d) -> p b d", b=NB)
        t1 = r1[:, :].rearrange("p (k s) -> p k s", k=KD)
        h2 = xin
        xs = r1[:, 0:D]
        ysb = r1[:, D:2 * D]
        bdn = r1[0:NE, 2 * D:3 * D]
        gT = r1[0:NE, 3 * D:3 * D + S]
        qk = r2[:, :].rearrange("p (j s) -> p j s", j=2 * QT)
        ya = r2[:, 0:4 * D].rearrange("p (k s) -> p k s", k=KD)
        x2 = r2[:, 0:4 * D].rearrange("p (b d) -> p b d", b=NB)
        bk_sb = r2[0:BUCKETS + 1, 0:(NSH + 2) * VEC]
        vec_sb = r2[0:NH, (NSH + 2) * VEC:2 * (NSH + 2) * VEC]
        g2b = r2[:, 4 * D:5 * D]
        tail = r2[:, 4 * D:6 * D]
        oh = tail[:, 0:512].rearrange("p (a e) -> p a e", e=NE)
        ohk = tail[:, 0:512].rearrange("p (b k e) -> p b k e", b=NB, k=TOPK)
        msk = tail[:, 512:640].rearrange("p (b e) -> p b e", b=NB)
        k4 = tail[:, 640:768].rearrange("p (b e) -> p b e", b=NB)
        gmat = tail[:, 768:896].rearrange("p (b e) -> p b e", b=NB)
        sg1 = tail[:, 896:1024].rearrange("p (b e) -> p b e", b=NB)
        lgt = tail[:, 1024:1152].rearrange("p (b e) -> p b e", b=NB)
        sg = tail[:, 1152:1152 + NB * NCOL].rearrange("p (b g) -> p b g", b=NB)
        lk = tail[:, 1344:1344 + NB * NCOL * 2].rearrange("p (b g c) -> p b g c", b=NB, c=2)
        top8 = tail[:, 1728:1760].rearrange("p (b k) -> p b k", b=NB)
        idxf = tail[:, 1760:1792].rearrange("p (b k) -> p b k", b=NB)
        idx8 = tail[:, 1792:1824].bitcast(U32).rearrange("p (b k) -> p b k", b=NB)
        gate = tail[:, 1824:1840].rearrange("p (b k) -> p b k", b=NB)
        eb = tail[:, 1840:1840 + NCOL]
        off32 = tail[:, 1888:1920]
        inc32 = tail[:, 1920:1952]
        nbk = tail[0:NE, 1952:1956]
        wr_sb = tail[:, 1152:1152 + KD * NE].rearrange("p (k e) -> p k e", k=KD)
        br_sb = tail[:, 1888:1920]
        tb1 = r3[:, 0:HPG * NSH * P].rearrange("p (h n) -> p h n", h=HPG)
        tb23 = r3[:, HPG * NSH * P:].rearrange("p (h g n) -> p h g n", h=HPG, g=2)
        bpart = r3[0:3 * NE, 0:D].bitcast(BF16)
        braw = r3[0:3 * NE, D:3 * D]
        btmp = r3[0:3 * NE, 3 * D:4 * D].bitcast(BF16)
        lgT = r3[0:NE, D + MAXBLK * P // 2:D + MAXBLK * P // 2 + S]
        sel = r3[0:3 * NE, D:D + MAXBLK * P // 2].bitcast(BF16).rearrange("p (g n) -> p g n", n=P)
        cu = work[:, 0:1024].rearrange("p (m s) -> p m s", m=2)
        yv = work[:, 1024:2048].rearrange("p (m s) -> p m s", m=2)
        prob = work[:, 2048:2816]
        pT = work[:, 2816:3584]
        relm = work[0:BUCKETS + 1, 3584:3584 + NH]
        stage = work[0:34 + KD, 3600:3728]
        h2T = work[:, :].rearrange("p (k s) -> p k s", k=KD)
        act = work[:, 0:1024].rearrange("p (m n) -> p m n", m=2)
        g1b, u1b, sgb = work[:, 1024:1536], work[:, 1536:2048], work[:, 2048:2560]
        hot = work[:, 2560:3072].rearrange("p (b n) -> p b n", b=NB)
        ov1 = work[:, 3072:3072 + MAXOVER * NE].rearrange("p (j e) -> p j e", e=NE)
        ov2 = work[:, 3584:3584 + MAXOVER * NE].rearrange("p (j e) -> p j e", e=NE)
        xTh, xTl = xT[:, 0:KD], xT[:, KD:2 * KD]
        aT = oT[:, :, :, :].rearrange("p a b (c n) -> p (a b c) n", n=P)
        aTh, aTl = aT[:, 0:KD], aT[:, KD:2 * KD]
        bk_A, bk_B, bk_D, bk_T = 0, 2, 4, 6

        x_in = [sem(f"x_in{b}") for b in range(NB)]
        c_in = sem("c_in")
        st_in = sem("st_in")
        bk_in = sem("bk_in")
        vec_out = sem("vec_out")
        tb_in = sem("tb_in")
        rawin = [sem(f"raw_in{r}") for r in range(RAW)]
        xraw_in = [sem(f"xraw_in{r}") for r in range(XRAW)]
        split_hi = sem("split_hi")
        split_lo = sem("split_lo")
        used = sem("used")
        relset = sem("relset")
        pe_small = sem("pe_small")
        small_rd = sem("small_rd")
        pe_vec = sem("pe_vec")
        vec_rd = sem("vec_rd")
        ssq = sem("ssq")
        eps_ok = sem("eps_ok")
        rstd_s = sem("rstd_s")
        xn_ok = sem("xn_ok")
        done = sem("done")
        freed = {"act": sem("freed_act"), "dve": sem("freed_dve")}
        hi_ok = sem("hi_ok")
        squares_ok = sem("squares_ok")
        scores_pe, logits_ok, negmax_ok, exp_ok, recip_ok, probs_ok = [
            sem(n) for n in ("scores_pe", "logits_ok", "negmax_ok", "exp_ok", "recip_ok", "probs_ok")]
        probsT_pe, probsT_a, probsT_d = [sem(n) for n in ("probsT_pe", "probsT_a", "probsT_d")]
        values_pe, oT_hi, oT_lo = [sem(n) for n in ("values_pe", "oT_hi", "oT_lo")]
        conv_ok, z_hi, z_lo = [sem(n) for n in ("conv_ok", "z_hi", "z_lo")]
        merged_ok, merged_hi, merged_lo = [sem(n) for n in ("merged_ok", "merged_hi", "merged_lo")]
        x2_in = sem("x2_in")
        g2_in = sem("g2_in")
        h2_ok = sem("h2_ok")
        h2_out = sem("h2_out")
        h2T_pe, h2T_a, h2T_d = sem("h2T_pe"), sem("h2T_a"), sem("h2T_d")
        logitsT_pe, logitsT_ok = sem("logitsT_pe"), sem("logitsT_ok")
        sum_ok, rstd2_ok = sem("sum_ok"), sem("rstd2_ok")
        wr_in = sem("wr_in")
        logit_rows_pe = sem("logit_rows_pe")
        gp_step = sem("gp_step")
        top4_ok, gate_exp_ok, chosen_ok, ranks_pe = [
            sem(n) for n in ("top4_ok", "gate_exp_ok", "chosen_ok", "ranks_pe")]
        blocks_ok, offsets_pe, tables_ok, over_ok = [
            sem(n) for n in ("blocks_ok", "offsets_pe", "tables_ok", "over_ok")]
        down_bias_in, gates_ok, gT_pe, gT_ok, down_bias_pe, x2_biased = [
            sem(n) for n in ("down_bias_in", "gates_ok", "gT_pe", "gT_ok", "down_bias_pe", "x2_biased")]
        bias_in, bias_parts_ok = sem("bias_in"), sem("bias_parts_ok")
        xs_set, ix_set = sem("xs_set"), sem("ix_set")
        chain = sem("chain")
        pchain = sem("pchain")
        column_ok = sem("column_ok")
        hot_ok = sem("hot_ok")
        turned_pe = sem("turned_pe")
        turned_read = sem("turned_read")
        turned_hi = sem("turned_hi")
        xs_in = sem("xs_in")
        gate_clamped, up_clamped, gate_up_ok, sigmoid_ok = [
            sem(n) for n in ("gate_clamped", "up_clamped", "gate_up_ok", "sigmoid_ok")]
        act_ok = sem("act_ok")
        y_ok = sem("y_ok")
        y_out = sem("y_out")
        rows_copied, rows_moved = sem("rows_copied"), sem("rows_moved")
        rows_free = sem("rows_free")
        final_in = [sem(f"final_in{n}") for n in range(2 * NB)]
        summed = sem("summed")
        out_stored = sem("out_stored")

        BEGIN, ACT0, ACT1, LOOKUP, ROWS0, ROWS1 = range(6)

        def tile(g, which):
            return 5 * g + (1 + which)

        def hi_tile(g, which):
            return 4 * g + (which if which < LOOKUP else which - 1)

        def unit_base(g):
            return UF if isinstance(g, int) and g == 0 else UPE * g + (UF - 8)

        w_in_v = w_in[0].rearrange("(k p) n -> p k n", p=P)
        w_bc_v = w_branch_conv[0].rearrange("(k p) n -> p k n", p=P)
        w_ba_v = w_branch_attn[0].rearrange("(k p) n -> p k n", p=P)
        w_out_v = w_out[0].rearrange("(k p) n -> p k n", p=P)
        x_v = x[0].rearrange("(i b) d -> i b d", b=NB)
        out_v = out[0].rearrange("(i b) d -> i b d", b=NB)
        h2_v = h2_dram.rearrange("(i b) d -> i b d", b=NB)
        y_v = y_dram.rearrange("(i b k) d -> i b k d", b=NB, k=TOPK)

        def front_source(c):
            name, i = CHUNKS[c]
            cols = slice(256 * i, 256 * i + 256)
            if name == "wba":
                return w_ba_v
            if name == "wbc":
                return w_bc_v[:, :, cols]
            if name == "wo":
                return w_out_v[:, :, cols]
            return w_in_v[:, :, IN_COL[name] + 256 * i:IN_COL[name] + 256 * i + 256]

        def raw_unit(n, slot):
            half = raw[:, slot, UH * (n % 2):UH * (n % 2) + UH]
            if n < UF and CHUNKS[n // 2][0] == "wba":
                return raw[:, slot, :].rearrange("p (k n) -> p k n", k=2)[:, :, 512 * (n % 2):512 * (n % 2) + 512]
            return half

        def expert_raw(g, c):
            q = c if isinstance(g, int) and g == 0 else c - 4
            slot = (q + RAW) % XRAW
            nth = (CPE // XRAW) * g + (q // XRAW + 1)
            return (raw[:, slot, :] if slot < RAW else more_raw[:, slot - RAW, :]), slot, nth

        def expert_unit(i, j):
            slot = j % XUN
            if slot < UN:
                return (w_hi, w_lo)[i][:, slot, :]
            return zT[:, i, 2 * (slot - UN):2 * (slot - UN) + 2, :].rearrange("p k s -> p (k s)")

        def packed(t, n):
            if n < UF and CHUNKS[n // 2][0] == "wba":
                return t[:, n % UN, :].rearrange("p (k n) -> p k n", k=2)
            return t[:, n % UN, :]

        def toeplitz(head, g):
            v0 = 0 if g == 0 else NSH + g - 1
            nv = NSH if g == 0 else 1
            base = vec_dram[head:head + 1, VEC * v0:VEC * v0 + 1]
            return bass.AP(base.tensor, base.offset, [[1, P], [VEC, nv], [1, P]])

        block = ctx.enter_context(nc.Block())

        @block.sync
        def _(sp):
            sp.dma_start(bk_sb, buckets).then_inc(bk_in, 16)
            sp.dma_start(relm[0:BUCKETS, :], rel_bias).then_inc(bk_in, 16)
            sp.dma_start(cst[:, :], consts).then_inc(c_in, 16)
            for b in range(NB):
                sp.dma_start(xin[:, b, :], x_v[:, b, :]).then_inc(x_in[b], 16)
            sp.dma_start(stage[0:8, :], norm1_g[0].rearrange("(k p) -> k p", p=P)).then_inc(st_in, 16)
            sp.dma_start(stage[34:34 + KD, :], norm2_g[0].rearrange("(k p) -> k p", p=P)).then_inc(st_in, 16)
            sp.dma_start(stage[8:32, :], conv_w[0].rearrange("t (k p) -> (t k) p", p=P)).then_inc(st_in, 16)
            for half in range(2):
                sp.dma_start(stage[32:33, DH * half:DH * half + DH], q_norm_g).then_inc(st_in, 16)
                sp.dma_start(stage[33:34, DH * half:DH * half + DH], k_norm_g).then_inc(st_in, 16)

            def load_front(c):
                if c >= RAW:
                    sp.wait_ge(split_lo, 2 * (c - RAW) + 2)
                dst = raw[:, c % RAW, :].rearrange("p (k n) -> p k n", k=2 if CHUNKS[c][0] == "wba" else KD)
                sp.dma_start(dst, front_source(c)).then_inc(rawin[c % RAW], 16)

            for c in range(RAW):
                load_front(c)
            sp.wait_ge(vec_rd, 5)
            sp.dma_start(vec_dram, vec_sb).then_inc(vec_out, 16)
            sp.wait_ge(vec_out, 16)
            for h in range(HPG):
                sp.dma_start(tb1[:, h, :].rearrange("p (v n) -> p v n", n=P), toeplitz(h, 0)).then_inc(tb_in, 16)
                for g in (1, 2):
                    sp.dma_start(tb23[:, h, g - 1:g, :], toeplitz(HPG * g + h, g)).then_inc(tb_in, 16)
            for c in range(RAW, NF):
                load_front(c)
                if CHUNKS[c] == ("gc", 1):
                    sp.wait_ge(logits_ok, HPG * NB)
                    for part in range(3):
                        sp.dma_start(braw[NE * part:NE * part + NE, :], b_gate_up[0]).then_inc(bias_in, 16)
                if CHUNKS[c] == ("wo", 3):
                    sp.wait_ge(merged_ok, KD)
                    for b in range(NB):
                        sp.dma_start(x2[:, b, :], x_v[:, b, :]).then_inc(x2_in, 16)
                    sp.dma_start(g2b, bass.AP(
                        norm2_g.tensor, norm2_g.offset, [[0, P], [1, D]])).then_inc(g2_in, 16)
                    sp.dma_start(wr_sb, w_router[0].rearrange("(k p) e -> p k e", p=P)).then_inc(wr_in, 16)
                    sp.dma_start(br_sb, bass.AP(b_router.tensor, b_router.offset, [[0, P], [1, NE]])).then_inc(wr_in, 16)

            def load_expert(g, c, e, first=False, what=None):
                dst, slot, _ = expert_raw(g, c)
                if not first:
                    sp.wait_ge(split_lo, unit_base(g) + (2 * c - 2 * XRAW + 2))
                c = c if what is None else what
                if c < 8:
                    half, k0 = c // 4, 2 * (c % 4)
                    src = w_gate_up[0][bass.ds(e, 1)].rearrange("o (p k) (s n) -> p (o k s) n", p=P, s=2)[
                        :, 2 * k0:2 * k0 + 4, 512 * half:512 * half + 512]
                    dst = dst.rearrange("p (a n) -> p a n", a=4)
                else:
                    half, k0 = (c - 8) // 2, 2 * (c % 2)
                    src = w_down[0][bass.ds(e, 1)].rearrange("o (h p k) n -> p (o h) k n", h=2, p=P)[
                        :, half, k0:k0 + 2, :]
                    dst = dst.rearrange("p (k n) -> p k n", k=2)
                sp.dma_start(dst, src).then_inc(xraw_in[slot], 16)

            sp.wait_ge(used, 2 * CHUNKS.index(("wo", 0)))
            for c in range(RAW):
                load_expert(0, c, 0, first=True)
            sp.wait_ge(split_lo, UF)
            for c in range(RAW, XRAW):
                load_expert(0, c, 0, first=True)
            sp.wait_ge(h2_ok, NB)
            for b in range(NB):
                sp.dma_start(h2_v[:, b, :], h2[:, b, :]).then_inc(h2_out, 16)
            for c in range(XRAW, 8):
                load_expert(0, c, 0)
            sp.wait_ge(h2T_pe, KD)
            sp.wait_ge(h2_out, 16 * NB)
            sp.dma_start(bdn, b_down[0]).then_inc(down_bias_in, 16)
            with sp.Fori(1, NE) as g:
                for c in range(CPE):
                    load_expert(g, c, g if c < 8 else g - 1)
            sp.wait_ge(over_ok, 1)
            sp.wait_ge(blocks_ok, 2)
            nblk = sp.value_load(ublk[0:1, NCOL:NCOL + 1], min_val=NE, max_val=MAXBLK)
            with sp.If(nblk > NE):
                with sp.Fori(NE, nblk) as g:
                    e = sp.value_load(ublk[0:1, bass.ds(g, 1)], min_val=0, max_val=NE - 1)
                    before = sp.value_load(ublk[0:1, bass.ds(g - 1, 1)], min_val=0, max_val=NE - 1)
                    for c in range(CPE):
                        load_expert(g, c, e if c < 8 else before)
            last_e = sp.value_load(ublk[0:1, bass.ds(nblk - 1, 1)], min_val=0, max_val=NE - 1)
            for c in range(4):
                load_expert(nblk, c, last_e, what=8 + c)
            sp.wait_ge(y_out, 16 * nblk)
            places = [raw[:, 0:2, :].rearrange("p a n -> p (a n)"),
                      more_raw[:, 0:2, :].rearrange("p a n -> p (a n)"), work[:, :], r3[:, 0:4 * D]]
            for b in range(NB):
                for k in range(0, TOPK, 2):
                    sp.dma_start(places[b][:, D * k:D * k + 2 * D].rearrange("p (k d) -> p k d", k=2),
                                 y_v[:, b, k:k + 2]).then_inc(final_in[2 * b + k // 2], 16)
            for b in range(NB):
                sp.wait_ge(summed, TOPK * (b + 1))
                sp.dma_start(out_v[:, b, :], x2[:, b, :]).then_inc(out_stored, 16)
            sp.wait_ge(out_stored, 16 * NB)

        @block.tensor
        def _(pe):
            def bank_free(ev):
                before = BEFORE[ev]
                if before is not None:
                    eng, n = FREED[before]
                    pe.wait_ge(freed[eng], n)

            def three(dst, a_hi, a_lo, b_hi, b_lo, start, stop):
                pe.matmul(dst, a_hi, b_hi, start=start, stop=False)
                pe.matmul(dst, a_hi, b_lo, start=False, stop=False)
                return pe.matmul(dst, a_lo, b_hi, start=False, stop=stop)

            pe.wait_ge(bk_in, 32)
            pe.wait_ge(relset, 1)
            nv = (NSH + 2) * VEC
            for j in range(5):
                w = min(512, nv - 512 * j)
                pe.matmul(ps[0:NH, j, 0:w], relm, bk_sb[:, 512 * j:512 * j + w],
                          start=True, stop=True).then_inc(pe_vec, 1)
            pe.wait_ge(c_in, 16)
            pe.wait_ge(st_in, 16 * 7)
            pe.transpose(ps[:, 7, 0:34 + KD], stage, ident[0:34 + KD, 0:34 + KD]).then_inc(pe_small, 1)
            pe.wait_ge(vec_rd, 5)
            pe.wait_ge(small_rd, 1)
            for b in range(NB):
                pe.wait_ge(xn_ok, b + 1)
            for k in range(KD):
                for b in range(NB):
                    last = pe.transpose(ps[:, k, P * b:P * b + P], xin[:, b, P * k:P * k + P], ident)
                last.then_inc(done, 1)

            def unit(n, tiles=(0, 1)):
                name, i = CHUNKS[n // 2]
                if 0 in tiles:
                    pe.wait_ge(split_lo, n + 1)
                wh, wl = w_hi[:, n % UN, :], w_lo[:, n % UN, :]
                h = n % 2
                if name == "wba":
                    wh = wh.rearrange("p (k n) -> p k n", k=2)
                    wl = wl.rearrange("p (k n) -> p k n", k=2)
                    pe.wait_ge(oT_lo, HPG * NB)
                    for m in range(4):
                        ev = EV[("wba", 4 * h + m)]
                        bank_free(ev)
                        c = slice(P * m, P * m + P)
                        for k in range(2):
                            last = three(ps[:, EVENTS[ev][2], :], wh[:, k, c], wl[:, k, c],
                                         oT[:, 0, k, :], oT[:, 1, k, :], k == 0, k == 1)
                    return last
                wh = wh.rearrange("p (k n) -> p k n", k=4)
                wl = wl.rearrange("p (k n) -> p k n", k=4)
                if name in ("v", "wo"):
                    src = hT if name == "v" else zT
                    for b in range(NB):
                        ev = EV[(name, 4 * i + b)]
                        if h == 0:
                            bank_free(ev)
                        for k in range(4):
                            kk = 4 * h + k
                            if name == "wo" and b == 0:
                                pe.wait_ge(merged_lo, kk + 1)
                            c = slice(P * b, P * b + P)
                            last = three(ps[:, EVENTS[ev][2], 0:256], src[:, 0, kk, c], src[:, 1, kk, c],
                                         wh[:, k, :], wl[:, k, :], kk == 0, kk == KD - 1)
                    return last
                src = zT if name == "wbc" else hT
                for m in tiles:
                    ev = EV[(name, 2 * i + m)]
                    if h == 0:
                        bank_free(ev)
                    for k in range(4):
                        kk = 4 * h + k
                        if m == 0:
                            pe.wait_ge(z_lo if name == "wbc" else freed["dve"], kk + 1)
                        c = slice(P * m, P * m + P)
                        last = three(ps[:, EVENTS[ev][2], :], wh[:, k, c], wl[:, k, c],
                                     src[:, 0, kk, :], src[:, 1, kk, :], kk == 0, kk == KD - 1)
                return last

            def square_sums(j):
                ev = EV[("ss", j)]
                bank_free(ev)
                pe.wait_ge(squares_ok, j + 1)
                pe.matmul(ps[:, EVENTS[ev][2], :], cst[:, C_BLK:C_BLK + P], yv[:, j % 2, :],
                          start=True, stop=True).then_inc(done, 1)

            def scores(u):
                hh, b = divmod(u, NB)
                half = slice(DH * (hh % 2), DH * (hh % 2) + DH)
                if u == 0:
                    pe.wait_ge(freed["dve"], FREED[EV[("k", QT - 1)]][1])
                    for bb in range(NB):
                        eng, n = FREED[EV[("v", 2 * NB + bb)]]
                        pe.wait_ge(freed[eng], n)
                else:
                    pe.wait_ge(logits_ok, u)
                for g in range(NG):
                    j = 2 * g + hh // 2
                    keys = slice(0, S) if g == 0 else slice(P * b, P * b + P)
                    dst = ps[:, 4, :] if g == 0 else ps[:, 5, P * (g - 1):P * g]
                    last = pe.matmul(dst, qk[half, j, P * b:P * b + P], qk[half, QT + j, keys],
                                     start=True, stop=True)
                last.then_inc(scores_pe, 1)

            def turn(u):
                pe.wait_ge(probs_ok, u + 1)
                if u:
                    pe.wait_ge(oT_lo, u)
                for c in range(6):
                    last = pe.transpose(ps[:, 6 + c // 4, P * (c % 4):P * (c % 4) + P],
                                        prob[:, P * c:P * c + P], ident)
                last.then_inc(probsT_pe, 1)

            def values(u):
                hh, b = divmod(u, NB)
                pe.wait_ge(probsT_a, u + 1)
                pe.wait_ge(probsT_d, u + 1)
                dst = ps[DH * (hh % 2):DH * (hh % 2) + DH, 7, 256:256 + P]
                for c in range(6):
                    g = 0 if c < 4 else c - 3
                    head = HPG * g + hh
                    last = pe.matmul(dst, v_sb[:, c if c < 4 else b, DH * head:DH * head + DH],
                                     pT[:, P * c:P * c + P], start=(c == 0), stop=(c == 5))
                last.then_inc(values_pe, 1)

            for kind, n in STEPS:
                if kind == "unit":
                    unit(n, (1,) if ("half", n) in STEPS else (0, 1)).then_inc(used, 1)
                elif kind == "half":
                    unit(n, (0,))
                elif kind == "ss":
                    square_sums(n)
                elif kind == "S":
                    scores(n)
                elif kind == "T":
                    turn(n)
                elif kind == "PV":
                    values(n)

            pe.wait_ge(freed["dve"], FREED[EV[("wo", 4 * NB - 1)]][1])
            for k in range(KD):
                for b in range(NB):
                    last = pe.transpose(ps[:, k, P * b:P * b + P], x2[:, b, P * k:P * k + P], ident)
                last.then_inc(h2T_pe, 1)
            pe.wait_ge(wr_in, 32)
            for k in range(KD):
                if k == 0:
                    pe.wait_ge(h2T_a, 1)
                    pe.wait_ge(h2T_d, 1)
                else:
                    pe.wait_ge(h2T_d if k % 2 else h2T_a, k // 2 + 1)
                last = pe.matmul(ps[0:NE, 0, :], wr_sb[:, k, :], h2T[:, k, :], start=(k == 0), stop=(k == KD - 1))
            last.then_inc(logitsT_pe, 1)
            pe.wait_ge(logitsT_ok, 1)
            for b in range(NB):
                last = pe.transpose(ps[:, 1, NE * b:NE * b + NE], lgT[:, P * b:P * b + P], ident[0:NE, 0:NE])
            last.then_inc(logit_rows_pe, 1)
            pe.wait_ge(chosen_ok, 1)
            pe.matmul(ps[:, 1, 0:P], cst[:, C_TRI:C_TRI + P], msk.rearrange("p b e -> p (b e)"),
                      start=True, stop=False)
            for c in range(NB - 1):
                later = NB - 1 - c
                last = pe.matmul(ps[:, 1, NE * (c + 1):P].rearrange("p (b e) -> p b e", b=later), ones,
                                 msk[:, c:c + 1, :].to_broadcast([P, later, NE]), start=False, stop=(c == NB - 2))
            last.then_inc(ranks_pe, 1)
            for b in range(NB):
                last = pe.matmul(ps[0:NE, 2, 0:1], msk[:, b, :], ones[:, 0:1], start=(b == 0), stop=(b == NB - 1))
            last.then_inc(ranks_pe, 1)
            def lookup(g):
                for b in range(NB):
                    last = pe.matmul(ps[:, bk_T, 0:2], hot[:, b, :], lk[:, b, bass.ds(g, 1), :],
                                     start=(b == 0), stop=(b == NB - 1))
                last.then_inc(turned_pe, 1)

            pe.wait_ge(hot_ok, NB)
            lookup(0)
            pe.wait_ge(blocks_ok, 1)
            nb_all = nbk[:, 3:4].to_broadcast([NE, P])
            pe.matmul(ps[:, 3, 0:NE], nb_all, cst[0:NE, C_TRI:C_TRI + NE], start=True, stop=True)
            pe.matmul(ps[:, 3, NE:2 * NE], nb_all, cst[0:NE, C_TRI:C_TRI + NE], start=True, stop=False)
            pe.matmul(ps[:, 3, NE:2 * NE], nb_all, ident[0:NE, 0:NE], start=False, stop=True).then_inc(offsets_pe, 1)

            def turn_rows(half):
                for k in range(4):
                    last = pe.transpose(ps[:, bk_T + half, P * k:P * k + P],
                                        xs[:, 4 * half + k::KD], ident)
                last.then_inc(turned_pe, 1)

            def turn_act(half):
                for k in range(4):
                    last = pe.transpose(ps[:, bk_T + half, P * k:P * k + P], act[:, half, k::4], ident)
                last.then_inc(turned_pe, 1)

            pe.wait_ge(xs_in, 16)
            turn_rows(0)
            turn_rows(1)
            pe.wait_ge(bias_parts_ok, 1)
            pe.wait_ge(blocks_ok, 2)
            nblk = pe.value_load(ublk[0:1, NCOL:NCOL + 1], min_val=NE, max_val=MAXBLK)

            def gate_up(g, j):
                half, k = divmod(j, 8)
                base = bk_A + 2 * half
                wh, wl = expert_unit(0, j), expert_unit(1, j)
                pe.wait_ge(split_lo, unit_base(g) + (j + 1))
                if k == 0:
                    for s in range(2):
                        pe.matmul(ps[:, base + s, :], sel[:, bass.ds(g, 1), :],
                                  bpart[:, D * s + 512 * half:D * s + 512 * half + 512],
                                  start=True, stop=False)
                for s in range(2):
                    c = slice(512 * s, 512 * s + 512)
                    last = three(ps[:, base + s, :], xTh[:, k, :], xTl[:, k, :], wh[:, c], wl[:, c],
                                 False, k == KD - 1)
                last.then_inc(used, 1)

            def down(g, pos, k):
                wh, wl = expert_unit(0, pos), expert_unit(1, pos)
                pe.wait_ge(split_lo, unit_base(g) + (pos + 1))
                for s in range(2):
                    c = slice(512 * s, 512 * s + 512)
                    last = three(ps[:, bk_D + s, :], aTh[:, k, :], aTl[:, k, :], wh[:, c], wl[:, c],
                                 k == 0, k == KD - 1)
                last.then_inc(used, 1)

            def next_rows(g, half):
                if half == 0:
                    pe.wait_ge(xs_in, 16 * g + 32)
                    pe.wait_ge(turned_read, tile(g, LOOKUP))
                turn_rows(half)

            pe.wait_ge(turned_read, tile(0, ACT1))
            for j in range(16):
                gate_up(0, j)
                if j == 6:
                    pe.wait_ge(hot_ok, 2 * NB)
                    lookup(1)
            next_rows(0, 0)
            next_rows(0, 1)
            with pe.Fori(1, nblk) as g:
                pe.wait_ge(turned_read, tile(g, BEGIN))
                for j in range(16):
                    if j == 8:
                        pe.wait_ge(act_ok, 2 * g + 1)
                    gate_up(g, j)
                    if j == 1:
                        pe.wait_ge(act_ok, 2 * g)
                        turn_act(0)
                    if j == 3:
                        pe.wait_ge(act_ok, 2 * g + 1)
                        turn_act(1)
                    if j == 6:
                        pe.wait_ge(hot_ok, NB * g + 2 * NB)
                        pe.wait_ge(turned_read, tile(g, ACT0))
                        lookup(g + 1)
                pe.wait_ge(y_ok, 2 * g)
                pe.wait_ge(turned_read, tile(g, ACT1))
                for k in range(KD):
                    down(g, 16 + k, k)
                    if k == 1:
                        next_rows(g, 0)
                    if k == 3:
                        next_rows(g, 1)
            pe.wait_ge(turned_read, tile(nblk, BEGIN))
            pe.wait_ge(act_ok, 2 * nblk)
            turn_act(0)
            pe.wait_ge(act_ok, 2 * nblk + 1)
            turn_act(1)
            pe.wait_ge(y_ok, 2 * nblk)
            pe.wait_ge(turned_read, tile(nblk, ACT1))
            for k in range(KD):
                down(nblk, k, k)

            pe.wait_ge(gates_ok, 1)
            for b in range(NB):
                last = pe.transpose(ps[0:NE, 0, P * b:P * b + P], gmat[:, b, :], ident)
            last.then_inc(gT_pe, 1)
            pe.wait_ge(gT_ok, 1)
            pe.wait_ge(down_bias_in, 16)
            for b in range(NB):
                if b >= 2:
                    pe.wait_ge(x2_biased, b - 1)
                for n in range(2):
                    last = pe.matmul(ps[:, 2 * (b % 2) + n, :], gT[:, P * b:P * b + P],
                                     bdn[:, 512 * n:512 * n + 512], start=True, stop=True)
                last.then_inc(down_bias_pe, 1)

        @block.scalar
        def _(sc):
            def split(n):
                sc.wait_ge(rawin[(n // 2) % RAW], 16 * (n // 2 // RAW + 1))
                if n >= UN:
                    sc.wait_ge(used, n - UN + 1)
                nc.scalar.activation(packed(w_hi, n), raw_unit(n, (n // 2) % RAW), ACT.Copy).then_inc(split_hi, 1)

            sc.wait_ge(eps_ok, 1)
            nc.scalar.activation(stat[:, 30:31], stat[:, 31:32], ACT.Sqrt)
            for b in range(NB):
                sc.wait_ge(x_in[b], 16)
                if b >= 2:
                    sc.wait_ge(ssq, b - 1)
                nc.scalar.activation(work[:, 0:D] if b % 2 == 0 else work[:, D:2 * D], xin[:, b, :], ACT.Square,
                                     accum_out=stat[:, b:b + 1]).then_inc(ssq, 1)
            sc.wait_ge(ssq, NB)
            nc.scalar.activation(stat[:, 4:8], stat[:, 0:4], ACT.Sqrt, scale=1.0 / D,
                                 bias=stat[:, 31:32]).then_inc(rstd_s, 1)
            for j in range(5):
                w = min(512, (NSH + 2) * VEC - 512 * j)
                sc.wait_ge(pe_vec, j + 1)
                nc.scalar.activation(vec_sb[:, 512 * j:512 * j + w], ps[0:NH, j, 0:w], ACT.Copy).then_inc(vec_rd, 1)
            for n in range(AHEAD):
                split(n)
            sc.wait_ge(small_rd, 1)
            for k in range(KD):
                sc.wait_ge(done, DONE[("xT", k)])
                nc.scalar.activation(hT[:, 0, k, :], ps[:, k, :], ACT.Copy, scale=small[:, k:k + 1]).then_inc(hi_ok, 1)

            for kind, n in STEPS:
                if kind == "unit":
                    if n + AHEAD < UF:
                        split(n + AHEAD)
                    name, i = CHUNKS[n // 2]
                    if name == "wba":
                        for m in range(4):
                            ev = EV[("wba", 4 * (n % 2) + m)]
                            sc.wait_ge(used, n + 1)
                            if n % 2 == 0 and m == 0:
                                sc.wait_ge(scores_pe, HPG * NB)
                            nc.scalar.activation(ya[:, 4 * (n % 2) + m, :], ps[:, EVENTS[ev][2], :],
                                                 ACT.Copy).then_inc(freed["act"], 1)
                    if n % 2 == 0:
                        continue
                    if name == "wo" and i == 3:
                        nc.scalar.activation(stat[:, 30:31], stat[:, 31:32], ACT.Sqrt)
                    if name == "wo":
                        for b in range(NB):
                            if i == 0 and b == 0:
                                sc.wait_ge(merged_lo, KD)
                            sc.wait_ge(freed["dve"], FREED[EV[("wo", NB * i + b)]][1])
                            if i or b:
                                sc.wait_ge(ssq, NB + NB * i + b)
                            nc.scalar.activation(work[:, 0:256], x2[:, b, 256 * i:256 * i + 256], ACT.Square,
                                                 accum_out=stat[:, 32 + NB * b + i:33 + NB * b + i]).then_inc(ssq, 1)
                        continue
                    for m in range(2):
                        t = 2 * i + m
                        if name in ("q", "k"):
                            j = t + (QT if name == "k" else 0)
                            ev = EV[(name, t)]
                            sc.wait_ge(used, n + 1)
                            if j >= 2:
                                sc.wait_ge(done, DONE[("ss", j - 2)])
                            nc.scalar.activation(yv[:, j % 2, :], ps[:, EVENTS[ev][2], :],
                                                 ACT.Square).then_inc(squares_ok, 1)
                        if name == "cc":
                            ev = EV[(name, t)]
                            sc.wait_ge(used, n + 1)
                            if t == 0:
                                sc.wait_ge(freed["dve"], FREED[EV[("k", QT - 1)]][1])
                            if t >= 2:
                                sc.wait_ge(conv_ok, t - 1)
                            nc.scalar.activation(cu[:, m, :], ps[:, EVENTS[ev][2], :],
                                                 ACT.Copy).then_inc(freed["act"], 1)
                        if name == "cb":
                            sc.wait_ge(freed["dve"], FREED[EV[(name, t)]][1])
                            nc.scalar.activation(zT[:, 0, t, :], yv[:, m, :], ACT.Copy).then_inc(z_hi, 1)
                        if name in ("gc", "ga"):
                            ev = EV[(name, t)]
                            sc.wait_ge(used, n + 1)
                            if name == "gc" and t < 2:
                                sc.wait_ge(z_lo, KD)
                            elif name == "gc":
                                sc.wait_ge(freed["dve"], FREED[EV[("wbc", t - 2)]][1])
                            elif t < 2:
                                sc.wait_ge(freed["dve"], FREED[EV[("wbc", KD - 1)]][1])
                            else:
                                sc.wait_ge(merged_lo, t - 1)
                            nc.scalar.activation(cu[:, m, :], ps[:, EVENTS[ev][2], :],
                                                 ACT.Sigmoid).then_inc(freed["act"], 1)
                        if name == "ga":
                            sc.wait_ge(merged_ok, t + 1)
                            nc.scalar.activation(zT[:, 0, t, :], cu[:, m, :], ACT.Copy).then_inc(merged_hi, 1)
                elif kind == "ss":
                    ev = EV[("ss", n)]
                    sc.wait_ge(done, DONE[("ss", n)])
                    if n >= 2:
                        j = n - 2
                        sc.wait_ge(freed["dve"], FREED[EV[("q", j) if j < QT else ("k", j - QT)]][1])
                    nc.scalar.activation(cu[:, n % 2, :], ps[:, EVENTS[ev][2], :], ACT.Sqrt,
                                         bias=stat[:, 31:32]).then_inc(freed["act"], 1)
                elif kind == "M":
                    sc.wait_ge(negmax_ok, n + 1)
                    nc.scalar.activation(prob, prob, ACT.Exp, bias=stat[:, 8:9],
                                         accum_out=stat[:, 9:10]).then_inc(exp_ok, 1)
                    sc.wait_ge(recip_ok, n + 1)
                    nc.scalar.activation(prob, prob, ACT.Copy, scale=stat[:, 11:12]).then_inc(probs_ok, 1)
                elif kind == "T":
                    sc.wait_ge(probsT_pe, n + 1)
                    nc.scalar.activation(pT[:, 0:512], ps[:, 6, :], ACT.Copy).then_inc(probsT_a, 1)
                elif kind == "PV":
                    hh, b = divmod(n, NB)
                    half = slice(DH * (hh % 2), DH * (hh % 2) + DH)
                    sc.wait_ge(values_pe, n + 1)
                    nc.scalar.activation(oT[half, 0, hh // 2, P * b:P * b + P][:, ::-1], ps[half, 7, 256:256 + P],
                                         ACT.Copy).then_inc(oT_hi, 1)

            def split_expert(g, pos):
                chunk, slot, nth = expert_raw(g, pos // 2)
                sc.wait_ge(xraw_in[slot], 16 * nth)
                sc.wait_ge(used, unit_base(g) + (pos - XUN + 1))
                nc.scalar.activation(expert_unit(0, pos), chunk[:, UH * (pos % 2):UH * (pos % 2) + UH],
                                     ACT.Copy).then_inc(split_hi, 1)

            sc.wait_ge(sum_ok, 1)
            nc.scalar.activation(stat[:, 16:20], stat[:, 12:16], ACT.Sqrt, scale=1.0 / D,
                                 bias=stat[:, 31:32]).then_inc(rstd_s, 1)
            for k in range(0, KD, 2):
                sc.wait_ge(h2T_pe, k + 1)
                nc.scalar.activation(h2T[:, k, :], ps[:, k, :], ACT.Copy,
                                     scale=small[:, 34 + k:35 + k]).then_inc(h2T_a, 1)
            for j in range(6):
                split_expert(0, j)
            sc.wait_ge(logitsT_pe, 1)
            sc.wait_ge(bias_parts_ok, 1)
            nc.scalar.activation(lgT, ps[0:NE, 0, :], ACT.Copy).then_inc(logitsT_ok, 1)
            sc.wait_ge(top4_ok, 1)
            nc.scalar.activation(gate, gate, ACT.Exp).then_inc(gate_exp_ok, 1)
            for j in range(6, XUN):
                split_expert(0, j)
            for half in range(2):
                sc.wait_ge(turned_pe, 2 + half)
                nc.scalar.activation(xTh[:, 4 * half:4 * half + 4, :],
                                     ps[:, bk_T + half, :].rearrange("p (k n) -> p k n", n=P),
                                     ACT.Copy).then_inc(turned_hi, 1)
            sc.wait_ge(blocks_ok, 2)
            sc.wait_ge(tables_ok, 1)
            nblk = sc.value_load(ublk[0:1, NCOL:NCOL + 1], min_val=NE, max_val=MAXBLK)

            def turned(g, which, dst, bank):
                sc.wait_ge(turned_pe, tile(g, which))
                nc.scalar.activation(dst, ps[:, bank, :].rearrange("p (k n) -> p k n", n=P),
                                     ACT.Copy).then_inc(turned_hi, 1)

            def sigmoid(g, half):
                sc.wait_ge(gate_clamped, 2 * g + half + 1)
                nc.scalar.activation(sgb, g1b, ACT.Sigmoid, scale=ALPHA).then_inc(sigmoid_ok, 1)

            def store_y(g, units, stored):
                sc.wait_ge(used, units)
                sc.wait_ge(rows_free, stored)
                for s in range(2):
                    nc.scalar.activation(ysb[:, 512 * s:512 * s + 512], ps[:, bk_D + s, :],
                                         ACT.Copy).then_inc(y_ok, 1)

            for j in range(XUN, 16):
                split_expert(0, j)
                if j == 12:
                    sigmoid(0, 0)
            turned(0, ROWS0, xTh[:, 0:4, :], bk_T)
            turned(0, ROWS1, xTh[:, 4:8, :], bk_T + 1)
            sigmoid(0, 1)
            with sc.Fori(1, nblk) as g:
                for j in range(UPE):
                    split_expert(g, j)
                    if j == 3:
                        store_y(g, unit_base(g), g)
                    if j == 5:
                        turned(g, ACT0, aTh[:, 0:4, :], bk_T)
                    if j == 7:
                        turned(g, ACT1, aTh[:, 4:8, :], bk_T + 1)
                    if j == 12:
                        sigmoid(g, 0)
                    if j == 20:
                        sigmoid(g, 1)
                    if j == 21:
                        turned(g, ROWS0, xTh[:, 0:4, :], bk_T)
                turned(g, ROWS1, xTh[:, 4:8, :], bk_T + 1)
            for pos in range(8):
                split_expert(nblk, pos)
                if pos == 1:
                    turned(nblk, ACT0, aTh[:, 0:4, :], bk_T)
                    turned(nblk, ACT1, aTh[:, 4:8, :], bk_T + 1)
                    store_y(nblk, unit_base(nblk), nblk)
            store_y(nblk, unit_base(nblk) + 8, nblk + 1)

        @block.vector
        def _(ve):
            links = [0]

            def link(ins):
                links[0] += 1
                ins.then_inc(chain, 1)
                ve.wait_ge(chain, links[0])

            def split(n):
                ve.wait_ge(split_hi, n + 1)
                nc.vector.tensor_tensor(packed(w_lo, n), raw_unit(n, (n // 2) % RAW), packed(w_hi, n).bitcast(F32),
                                        ALU.subtract).then_inc(split_lo, 1)

            nc.vector.memset(stat[:, 31:32], EPS).then_inc(eps_ok, 1)
            nc.vector.memset(uix[:, :], 0).then_inc(ix_set, 1)
            nc.vector.memset(relm[BUCKETS:BUCKETS + 1, :], 1.0).then_inc(relset, 1)
            ve.wait_ge(pe_small, 1)
            link(nc.vector.tensor_copy(small[:, :], ps[:, 7, 0:34 + KD]))
            nc.vector.tensor_scalar(small[:, 32:33], small[:, 32:33], DH ** -0.5, None, ALU.mult).then_inc(small_rd, 1)
            ve.wait_ge(rstd_s, 1)
            link(nc.vector.reciprocal(stat[:, 4:8], stat[:, 4:8]))
            for b in range(NB):
                nc.vector.tensor_scalar(xin[:, b, :], xin[:, b, :], stat[:, 4 + b:5 + b], None,
                                        ALU.mult).then_inc(xn_ok, 1)
            for n in range(AHEAD):
                split(n)
            ve.wait_ge(small_rd, 1)
            for k in range(KD):
                ve.wait_ge(hi_ok, k + 1)
                nc.vector.scalar_tensor_tensor(hT[:, 1, k, :], ps[:, k, :], small[:, k:k + 1],
                                               hT[:, 0, k, :].bitcast(F32), ALU.mult,
                                               ALU.subtract).then_inc(freed["dve"], 1)

            def convolve(m, t):
                u, y = cu[:, m, :], yv[:, m, :]
                tap = [small[:, 8 + KD * i + t:9 + KD * i + t] for i in range(3)]
                link(nc.vector.tensor_scalar(y, u, tap[2], None, ALU.mult))

                def add(dst, src, w):
                    link(nc.vector.scalar_tensor_tensor(dst, src, w, dst, ALU.mult, ALU.add))

                add(y[:, P:S], u[:, 0:S - P], tap[1])
                add(y[:, 1:P], u[:, S - P:S - 1], tap[1])
                add(y[:, 2 * P:S], u[:, 0:S - 2 * P], tap[0])
                y2, u2 = [a.rearrange("p (b n) -> p b n", b=NB) for a in (y, u)]
                nc.vector.scalar_tensor_tensor(y2[:, 0:2, 1:P], u2[:, 2:4, 0:P - 1], tap[0], y2[:, 0:2, 1:P],
                                               ALU.mult, ALU.add).then_inc(conv_ok, 1)

            for kind, n in STEPS:
                if kind == "unit":
                    if n + AHEAD < UF:
                        split(n + AHEAD)
                    name, i = CHUNKS[n // 2]
                    if name == "cb" and n % 2 == 0:
                        convolve(1, 2 * i + 1)
                    if n % 2 == 0:
                        continue
                    if name in ("v", "wo"):
                        for b in range(NB):
                            ev = EV[(name, NB * i + b)]
                            ve.wait_ge(used, n + 1)
                            src = ps[:, EVENTS[ev][2], 0:256]
                            if name == "v":
                                nc.vector.tensor_copy(v_sb[:, b, 256 * i:256 * i + 256], src).then_inc(freed["dve"], 1)
                            else:
                                dst = x2[:, b, 256 * i:256 * i + 256]
                                if b == 0:
                                    ve.wait_ge(x2_in, 16 * NB)
                                    ve.wait_ge(merged_lo, KD)
                                nc.vector.tensor_tensor(dst, src, dst, ALU.add).then_inc(freed["dve"], 1)
                        continue
                    for m in range(2):
                        t = 2 * i + m
                        if name == "cx":
                            ev = EV[(name, t)]
                            ve.wait_ge(freed["act"], FREED[EV[("cc", t)]][1])
                            ve.wait_ge(used, n + 1)
                            nc.vector.tensor_tensor(cu[:, m, :], cu[:, m, :], ps[:, EVENTS[ev][2], :],
                                                    ALU.mult).then_inc(freed["dve"], 1)
                        if name == "cx" and m == 1:
                            ve.wait_ge(freed["dve"], FREED[ev][1])
                            if t >= 2:
                                ve.wait_ge(z_hi, t - 1)
                            convolve(0, t - 1)
                        if name == "cb":
                            ev = EV[(name, t)]
                            ve.wait_ge(used, n + 1)
                            ve.wait_ge(conv_ok, t + 1)
                            nc.vector.tensor_tensor(yv[:, m, :], yv[:, m, :], ps[:, EVENTS[ev][2], :],
                                                    ALU.mult).then_inc(freed["dve"], 1)
                            ve.wait_ge(z_hi, t + 1)
                            nc.vector.tensor_tensor(zT[:, 1, t, :], yv[:, m, :], zT[:, 0, t, :].bitcast(F32),
                                                    ALU.subtract).then_inc(z_lo, 1)
                        if name == "wbc":
                            ev = EV[(name, t)]
                            ve.wait_ge(used, n + 1)
                            ve.wait_ge(freed["act"], FREED[EV[("gc", t)]][1])
                            if t == 0:
                                ve.wait_ge(values_pe, HPG * NB)
                            nc.vector.tensor_tensor(t1[:, t, :], cu[:, m, :], ps[:, EVENTS[ev][2], :],
                                                    ALU.mult).then_inc(freed["dve"], 1)
                        if name == "ga":
                            ve.wait_ge(freed["act"], FREED[EV[("ga", t)]][1])
                            link(nc.vector.tensor_tensor(cu[:, m, :], cu[:, m, :], ya[:, t, :], ALU.mult))
                            nc.vector.tensor_tensor(cu[:, m, :], cu[:, m, :], t1[:, t, :], ALU.add).then_inc(merged_ok, 1)
                            ve.wait_ge(merged_hi, t + 1)
                            nc.vector.tensor_tensor(zT[:, 1, t, :], cu[:, m, :], zT[:, 0, t, :].bitcast(F32),
                                                    ALU.subtract).then_inc(merged_lo, 1)
                elif kind == "ss":
                    j = n
                    proj = EV[("q", j) if j < QT else ("k", j - QT)]
                    ve.wait_ge(freed["act"], FREED[EV[("ss", j)]][1])
                    link(nc.vector.reciprocal(cu[:, j % 2, :], cu[:, j % 2, :]))
                    if j == 0:
                        ve.wait_ge(vec_out, 16)
                    g = small[:, 32:33] if j < QT else small[:, 33:34]
                    dst, a, b = [t.rearrange("p (b n) -> p b n", b=NB) for t in (
                        qk[:, j, :], ps[:, EVENTS[proj][2], :], cu[:, j % 2, :])]
                    if j < QT:
                        dst = dst[:, :, ::-1]
                    nc.vector.scalar_tensor_tensor(dst, a, g, b, ALU.mult, ALU.mult).then_inc(freed["dve"], 1)
                elif kind == "M":
                    hh, b = divmod(n, NB)
                    if n == 0:
                        ve.wait_ge(tb_in, 16 * NH)
                    else:
                        ve.wait_ge(probsT_pe, n)
                    ve.wait_ge(scores_pe, n + 1)
                    lo = P * (NB - 1 - b)
                    nc.vector.tensor_tensor(prob[:, 0:512], ps[:, 4, :], tb1[:, hh, lo:lo + 512], ALU.add)
                    link(nc.vector.tensor_tensor(prob[:, 512:768], ps[:, 5, 0:256],
                                                 tb23[:, hh].rearrange("p g n -> p (g n)"), ALU.add))
                    nc.vector.tensor_reduce(stat[:, 10:11], prob, AX.X, ALU.max).then_inc(logits_ok, 1)
                    ve.wait_ge(logits_ok, n + 1)
                    nc.vector.tensor_scalar(stat[:, 8:9], stat[:, 10:11], -1.0, None, ALU.mult).then_inc(negmax_ok, 1)
                    ve.wait_ge(exp_ok, n + 1)
                    nc.vector.reciprocal(stat[:, 11:12], stat[:, 9:10]).then_inc(recip_ok, 1)
                elif kind == "T":
                    ve.wait_ge(probsT_pe, n + 1)
                    nc.vector.tensor_copy(pT[:, 512:768], ps[:, 7, 0:256]).then_inc(probsT_d, 1)
                elif kind == "PV":
                    hh, b = divmod(n, NB)
                    half = slice(DH * (hh % 2), DH * (hh % 2) + DH)
                    ve.wait_ge(oT_hi, n + 1)
                    hi, lo = [oT[half, i, hh // 2, P * b:P * b + P][:, ::-1] for i in range(2)]
                    nc.vector.tensor_tensor(lo, ps[half, 7, 256:256 + P], hi.bitcast(F32),
                                            ALU.subtract).then_inc(oT_lo, 1)

            def split_expert(g, pos):
                chunk, _, _ = expert_raw(g, pos // 2)
                ve.wait_ge(split_hi, unit_base(g) + (pos + 1))
                nc.vector.tensor_tensor(expert_unit(1, pos), chunk[:, UH * (pos % 2):UH * (pos % 2) + UH],
                                        expert_unit(0, pos).bitcast(F32), ALU.subtract).then_inc(split_lo, 1)

            ve.wait_ge(ssq, NB + 4 * NB)
            nc.vector.tensor_reduce(stat[:, 12:16], stat[:, 32:32 + 4 * NB].rearrange("p (b i) -> p b i", b=NB),
                                    AX.X, ALU.add).then_inc(sum_ok, 1)

            def half_turned(k):
                ve.wait_ge(h2T_pe, k + 1)
                nc.vector.tensor_scalar(h2T[:, k, :], ps[:, k, :], small[:, 34 + k:35 + k], None,
                                        ALU.mult).then_inc(h2T_d, 1)

            half_turned(1)
            ve.wait_ge(rstd_s, 2)
            nc.vector.reciprocal(stat[:, 16:20], stat[:, 16:20]).then_inc(rstd2_ok, 1)
            for k in range(3, KD, 2):
                half_turned(k)
            ve.wait_ge(g2_in, 16)
            ve.wait_ge(rstd2_ok, 1)
            for b in range(NB):
                nc.vector.scalar_tensor_tensor(h2[:, b, :], x2[:, b, :], stat[:, 16 + b:17 + b], g2b,
                                               ALU.mult, ALU.mult).then_inc(h2_ok, 1)
            for j in range(2):
                split_expert(0, j)
            ve.wait_ge(logit_rows_pe, 1)
            for b in range(NB):
                last = nc.vector.scalar_tensor_tensor(lgt[:, b, :], ps[:, 1, NE * b:NE * b + NE],
                                                      stat[:, 16 + b:17 + b], br_sb, ALU.mult, ALU.add)
            link(last)
            for b in range(NB):
                link(nc.vector.max(top8[:, b, :], lgt[:, b, :]))
                link(nc.vector.max_index(idx8[:, b, :], top8[:, b, :], lgt[:, b, :]))
            link(nc.vector.tensor_scalar(idxf[:, :, 0:TOPK], idx8[:, :, 0:TOPK], 1.0, None, ALU.add))
            for b in range(NB):
                nc.vector.tensor_tensor(ohk[:, b], idxf[:, b, 0:TOPK].unsqueeze(2).to_broadcast([P, TOPK, NE]),
                                        cst[:, C_IOTA:C_IOTA + NE].unsqueeze(1).to_broadcast([P, TOPK, NE]),
                                        ALU.is_equal)
            nc.vector.tensor_tensor(gate, top8[:, :, 0:TOPK], top8[:, :, 0:1].to_broadcast([P, NB, TOPK]),
                                    ALU.subtract).then_inc(top4_ok, 1)
            ve.wait_ge(top4_ok, 1)
            nc.vector.tensor_reduce(msk, ohk.rearrange("p b k e -> p b e k"), AX.X, ALU.add).then_inc(chosen_ok, 1)
            link(nc.vector.scalar_tensor_tensor(k4, ohk[:, :, 2, :], 2.0, ohk[:, :, 1, :], ALU.mult, ALU.add))
            link(nc.vector.scalar_tensor_tensor(k4, ohk[:, :, 3, :], 3.0, k4, ALU.mult, ALU.add))
            for b in range(NB):
                nc.vector.tensor_scalar(lk[:, b, 0:NE, 1], k4[:, b, :], cst[:, C_TOK4 + b:C_TOK4 + b + 1], None,
                                        ALU.add)
                last = nc.vector.tensor_scalar(lk[:, b, :, 0], cst[:, C_ONE:C_ONE + NCOL],
                                               cst[:, C_TOK + b:C_TOK + b + 1], None, ALU.mult)
            link(last)
            ve.wait_ge(ranks_pe, 1)
            ve.wait_ge(chosen_ok, 1)
            link(nc.vector.scalar_tensor_tensor(sg1, ps[:, 1, 0:P].rearrange("p (b e) -> p b e", b=NB), 1.0, msk,
                                                ALU.add, ALU.mult))
            for b in range(NB):
                nc.vector.tensor_scalar(hot[:, b, :], cst[:, C_IOTA:C_IOTA + P], sg1[:, b, 0:1], None,
                                        ALU.is_equal).then_inc(hot_ok, 1)
            nc.vector.tensor_copy(sg[:, :, 0:NE], sg1).then_inc(tables_ok, 1)
            ve.wait_ge(ranks_pe, 2)
            link(nc.vector.tensor_scalar(nbk[:, 0:1], ps[0:NE, 2, 0:1], P + 0.5, None, ALU.is_gt))
            link(nc.vector.tensor_scalar(nbk[:, 1:2], ps[0:NE, 2, 0:1], 2 * P + 0.5, None, ALU.is_gt))
            link(nc.vector.tensor_scalar(nbk[:, 2:3], ps[0:NE, 2, 0:1], 3 * P + 0.5, None, ALU.is_gt))
            link(nc.vector.tensor_tensor(nbk[:, 0:1], nbk[:, 0:1], nbk[:, 1:2], ALU.add))
            nc.vector.tensor_tensor(nbk[:, 3:4], nbk[:, 0:1], nbk[:, 2:3], ALU.add).then_inc(blocks_ok, 1)

            ve.wait_ge(turned_pe, 1)
            ve.wait_ge(ix_set, 1)
            nc.vector.tensor_scalar(uix[:, 0:2], ps[:, bk_T, 0:2], float(OUT_OF_RANGE), None,
                                    ALU.add).then_inc(turned_read, 1)
            ve.wait_ge(turned_read, 1)
            nc.vector.tensor_copy(uix[:, 2:3], uix[:, 1:2]).then_inc(rows_moved, 1)
            for j in range(2, 4):
                split_expert(0, j)
            ve.wait_ge(offsets_pe, 1)
            nc.vector.tensor_copy(off32, ps[:, 3, 0:NE])
            link(nc.vector.tensor_copy(inc32, ps[:, 3, NE:2 * NE]))
            nc.vector.tensor_scalar(ublk[:, NCOL + 1:NCOL + 2], ps[:, 3, 2 * NE - 1:2 * NE], float(NE - 1), None,
                                    ALU.add)
            nc.vector.tensor_scalar(ublk[:, NCOL:NCOL + 1], ps[:, 3, 2 * NE - 1:2 * NE], float(NE), None,
                                    ALU.add).then_inc(blocks_ok, 1)
            for j in range(4, 6):
                split_expert(0, j)
            for half in range(2):
                ve.wait_ge(turned_hi, half + 1)
                dst = xTl[:, 4 * half:4 * half + 4, :]
                nc.vector.tensor_tensor(dst, ps[:, bk_T + half, :].rearrange("p (k n) -> p k n", n=P),
                                        xTh[:, 4 * half:4 * half + 4, :].bitcast(F32),
                                        ALU.subtract).then_inc(turned_read, 1)
            ve.wait_ge(blocks_ok, 2)
            nblk = ve.value_load(ublk[0:1, NCOL:NCOL + 1], min_val=NE, max_val=MAXBLK)

            def activate(g, half):
                bank = bk_A + 2 * half
                ve.wait_ge(used, unit_base(g) + (8 * half + 8))
                nc.vector.tensor_scalar(g1b, ps[:, bank, :], LIMIT, None, ALU.min).then_inc(gate_clamped, 1)
                nc.vector.tensor_scalar(u1b, ps[:, bank + 1, :], LIMIT, -LIMIT, ALU.min,
                                        ALU.max).then_inc(up_clamped, 1)
                ve.wait_ge(up_clamped, 2 * g + (half + 1))
                nc.vector.scalar_tensor_tensor(u1b, u1b, 1.0, g1b, ALU.add, ALU.mult).then_inc(gate_up_ok, 1)
                ve.wait_ge(gate_up_ok, 2 * g + (half + 1))
                ve.wait_ge(sigmoid_ok, 2 * g + (half + 1))
                ve.wait_ge(turned_pe, tile(g, ACT0 + half))
                nc.vector.tensor_tensor(act[:, half, :], u1b, sgb, ALU.mult).then_inc(act_ok, 1)

            def turned(g, which, hi, lo, bank):
                ve.wait_ge(turned_hi, hi_tile(g, which))
                nc.vector.tensor_tensor(lo, ps[:, bank, :].rearrange("p (k n) -> p k n", n=P), hi.bitcast(F32),
                                        ALU.subtract).then_inc(turned_read, 1)

            def row_numbers(g):
                ve.wait_ge(turned_pe, tile(g, LOOKUP))
                ve.wait_ge(rows_moved, g + 1)
                nc.vector.tensor_scalar(uix[:, 0:2], ps[:, bk_T, 0:2], float(OUT_OF_RANGE), None,
                                        ALU.add).then_inc(turned_read, 1)

            def shift_rows(g):
                ve.wait_ge(rows_free, g + 1)
                ve.wait_ge(turned_read, tile(g, LOOKUP))
                nc.vector.tensor_copy(ushift[:, :], uix[:, 1:4]).then_inc(rows_copied, 1)
                ve.wait_ge(rows_copied, g + 1)
                nc.vector.tensor_copy(uix[:, 2:5], ushift[:, :]).then_inc(rows_moved, 1)

            ve.sem_inc(act_ok, 1)
            def gates():
                ve.wait_ge(gate_exp_ok, 1)
                link(nc.vector.tensor_reduce(stat[:, 20:24], gate, AX.X, ALU.add))
                link(nc.vector.reciprocal(stat[:, 20:24], stat[:, 20:24]))
                link(nc.vector.tensor_tensor(gate, gate, stat[:, 20:24].unsqueeze(2).to_broadcast([P, NB, TOPK]),
                                             ALU.mult))
                for b in range(NB):
                    last = nc.vector.tensor_tensor(ohk[:, b], ohk[:, b],
                                                   gate[:, b, :].unsqueeze(2).to_broadcast([P, TOPK, NE]), ALU.mult)
                link(last)
                nc.vector.tensor_reduce(gmat, ohk.rearrange("p b k e -> p b e k"), AX.X, ALU.add).then_inc(gates_ok, 1)

            for j in range(6, 16):
                split_expert(0, j)
                if j == 6:
                    gates()
                if j == 9:
                    row_numbers(0)
                if j == 12:
                    activate(0, 0)
                if j == 14:
                    shift_rows(0)
            turned(0, ROWS0, xTh[:, 0:4, :], xTl[:, 0:4, :], bk_T)
            turned(0, ROWS1, xTh[:, 4:8, :], xTl[:, 4:8, :], bk_T + 1)
            activate(0, 1)
            with ve.Fori(1, nblk) as g:
                for j in range(UPE):
                    split_expert(g, j)
                    if j == 5:
                        turned(g, ACT0, aTh[:, 0:4, :], aTl[:, 0:4, :], bk_T)
                    if j == 7:
                        turned(g, ACT1, aTh[:, 4:8, :], aTl[:, 4:8, :], bk_T + 1)
                    if j == 9:
                        row_numbers(g)
                    if j == 12:
                        activate(g, 0)
                    if j == 16:
                        shift_rows(g)
                    if j == 20:
                        activate(g, 1)
                    if j == 21:
                        turned(g, ROWS0, xTh[:, 0:4, :], xTl[:, 0:4, :], bk_T)
                turned(g, ROWS1, xTh[:, 4:8, :], xTl[:, 4:8, :], bk_T + 1)
            for pos in range(8):
                split_expert(nblk, pos)
                if pos == 1:
                    turned(nblk, ACT0, aTh[:, 0:4, :], aTl[:, 0:4, :], bk_T)
                    turned(nblk, ACT1, aTh[:, 4:8, :], aTl[:, 4:8, :], bk_T + 1)

            ve.wait_ge(gT_pe, 1)
            nc.vector.tensor_copy(gT, ps[0:NE, 0, :]).then_inc(gT_ok, 1)
            for b in range(NB):
                ve.wait_ge(down_bias_pe, b + 1)
                nc.vector.tensor_tensor(x2[:, b, :], x2[:, b, :],
                                        ps[:, 2 * (b % 2):2 * (b % 2) + 2, :].rearrange("p a n -> p (a n)"),
                                        ALU.add).then_inc(x2_biased, 1)
            ve.wait_ge(x2_biased, NB)
            places = [raw[:, 0:2, :].rearrange("p a n -> p (a n)"),
                      more_raw[:, 0:2, :].rearrange("p a n -> p (a n)"), work[:, :], r3[:, 0:4 * D]]
            for b in range(NB):
                for k in range(TOPK):
                    if k % 2 == 0:
                        ve.wait_ge(final_in[2 * b + k // 2], 16)
                    nc.vector.scalar_tensor_tensor(x2[:, b, :], places[b][:, D * k:D * k + D], gate[:, b, k:k + 1],
                                                   x2[:, b, :], ALU.mult, ALU.add).then_inc(summed, 1)
                    if k + 1 < TOPK:
                        ve.wait_ge(summed, TOPK * b + k + 1)

        @block.gpsimd
        def _(gp):
            links = [0]

            def link(ins):
                links[0] += 1
                ins.then_inc(pchain, 1)
                gp.wait_ge(pchain, links[0])

            gp.sem_inc(rows_free, 2)
            gp.wait_ge(bias_in, 16 * 3)
            gp.wait_ge(c_in, 16)
            link(nc.gpsimd.tensor_copy(bpart, braw))
            link(nc.gpsimd.tensor_tensor(braw, braw, bpart, ALU.subtract))
            link(nc.gpsimd.tensor_copy(btmp, braw))
            link(nc.gpsimd.tensor_copy(bpart[NE:2 * NE, :], btmp[NE:2 * NE, :]))
            link(nc.gpsimd.tensor_tensor(braw, braw, btmp, ALU.subtract))
            nc.gpsimd.tensor_copy(bpart[2 * NE:3 * NE, :], braw[2 * NE:3 * NE, :]).then_inc(bias_parts_ok, 1)
            gp.wait_ge(bias_parts_ok, 1)
            link(nc.gpsimd.tensor_scalar(
                sel[:, 0:NE, :], cst[0:3 * NE, C_IOTA:C_IOTA + NE].unsqueeze(2).to_broadcast([3 * NE, NE, P]),
                cst[0:3 * NE, C_RMOD:C_RMOD + 1], None, ALU.is_equal))
            gp.wait_ge(h2_out, 16 * NB)
            gp.wait_ge(h2T_pe, KD)
            nc.gpsimd.memset(xs, 0.0).then_inc(xs_set, 1)

            last_token, last_row = gp.to_reg(S - 1), gp.to_reg(S * TOPK - 1)

            def slots(g):
                nc.gpsimd.tensor_copy(stat[:, 24:28], sg[:, :, bass.ds(g, 1)].rearrange("p b o -> p (b o)")
                                      ).then_inc(column_ok, 1)
                gp.wait_ge(column_ok, g)
                gp.sem_inc(gp_step, 1)
                for b in range(NB):
                    nc.gpsimd.tensor_scalar(hot[:, b, :], cst[:, C_IOTA:C_IOTA + P], stat[:, 24 + b:25 + b], None,
                                            ALU.is_equal).then_inc(hot_ok, 1)

            def gather():
                nc.gpsimd.indirect_dma_start(
                    out=xs, out_offset=None, in_=h2_dram,
                    in_offset=bass.IndirectOffsetOnAxis(ap=uix[:, 0:1], axis=0),
                    bounds_check=last_token, oob_is_err=False).then_inc(xs_in, 16)

            gp.wait_ge(tables_ok, 1)
            gp.wait_ge(xs_set, 1)
            gp.wait_ge(turned_read, 1)
            gather()

            jrow = cst[:, C_IOTA:C_IOTA + MAXOVER].unsqueeze(2).to_broadcast([P, MAXOVER, NE])
            erow = cst[:, C_IOTA:C_IOTA + NE].unsqueeze(1).to_broadcast([P, MAXOVER, NE])
            off_b = off32.unsqueeze(1).to_broadcast([P, MAXOVER, NE])
            inc_b = inc32.unsqueeze(1).to_broadcast([P, MAXOVER, NE])
            over = slice(NE, MAXBLK)

            def total(dst, src):
                w = NE
                while w > 2:
                    w //= 2
                    link(nc.gpsimd.tensor_tensor(src[:, :, 0:w], src[:, :, 0:w], src[:, :, w:2 * w], ALU.add))
                link(nc.gpsimd.tensor_tensor(dst, src[:, :, 0], src[:, :, 1], ALU.add))

            def over_experts():
                link(nc.gpsimd.tensor_tensor(ov1, jrow, off_b, ALU.subtract))
                link(nc.gpsimd.tensor_scalar(ov1, ov1, 0.5, None, ALU.is_gt))
                link(nc.gpsimd.tensor_tensor(ov2, jrow, inc_b, ALU.subtract))
                link(nc.gpsimd.tensor_scalar(ov2, ov2, 0.5, None, ALU.is_lt))
                link(nc.gpsimd.tensor_tensor(ov1, ov1, ov2, ALU.mult))
                link(nc.gpsimd.tensor_tensor(ov2, ov1, erow, ALU.mult))
                link(nc.gpsimd.tensor_copy(eb[:, 0:NE], cst[:, C_IOTA:C_IOTA + NE]))
                link(nc.gpsimd.memset(eb[:, MAXBLK:NCOL], 1.0))
                link(nc.gpsimd.memset(sg[:, :, MAXBLK:NCOL], 0.0))
                link(nc.gpsimd.memset(lk[:, :, MAXBLK:NCOL, 1], 0.0))
                total(eb[:, over], ov2)

            def over_slots(b):
                link(nc.gpsimd.tensor_tensor(ov2, off_b, jrow, ALU.subtract))
                link(nc.gpsimd.tensor_scalar(ov2, ov2, float(P), None, ALU.mult))
                link(nc.gpsimd.tensor_tensor(ov2, ov2, sg1[:, b, :].unsqueeze(1).to_broadcast([P, MAXOVER, NE]),
                                             ALU.add))
                link(nc.gpsimd.tensor_tensor(ov2, ov2, ov1, ALU.mult))
                total(sg[:, b, over], ov2)
                link(nc.gpsimd.tensor_tensor(ov2, ov1, k4[:, b, :].unsqueeze(1).to_broadcast([P, MAXOVER, NE]),
                                             ALU.mult))
                total(lk[:, b, over, 1], ov2)
                link(nc.gpsimd.tensor_scalar(lk[:, b, over, 1], lk[:, b, over, 1],
                                             cst[:, C_TOK4 + b:C_TOK4 + b + 1], None, ALU.add))

            def over_selectors():
                link(nc.gpsimd.tensor_scalar(sel[:, over, :], eb[0:3 * NE, over].unsqueeze(2).to_broadcast(
                    [3 * NE, MAXOVER, P]), cst[0:3 * NE, C_RMOD:C_RMOD + 1], None, ALU.is_equal))
                link(nc.gpsimd.tensor_scalar(eb, eb, 1.0, -1.0, ALU.max, ALU.add))
                nc.gpsimd.tensor_copy(ublk[:, 0:NCOL], eb).then_inc(over_ok, 1)
                gp.wait_ge(over_ok, 1)

            gp.wait_ge(blocks_ok, 2)
            nblk = gp.value_load(ublk[0:1, NCOL:NCOL + 1], min_val=NE, max_val=MAXBLK)
            but_one = gp.value_load(ublk[0:1, NCOL + 1:NCOL + 2], min_val=NE - 1, max_val=MAXBLK - 1)

            def next_slots(g):
                gp.wait_ge(turned_pe, tile(0, ACT1) if isinstance(g, int) and g == 0 else tile(g, BEGIN))
                slots(g + 1)

            def gather_next(g):
                gp.wait_ge(turned_read, tile(g, LOOKUP))
                gp.sem_inc(gp_step, 1)
                gather()

            def scatter(g, col, outputs):
                gp.wait_ge(y_ok, outputs)
                gp.wait_ge(rows_moved, g + 1)
                gp.sem_inc(gp_step, 1)
                nc.gpsimd.indirect_dma_start(
                    out=y_dram, out_offset=bass.IndirectOffsetOnAxis(ap=uix[:, col:col + 1], axis=0),
                    in_=ysb, in_offset=None, bounds_check=last_row, oob_is_err=False).then_inc(y_out, 16)

            def stored(blocks):
                gp.wait_ge(y_out, 16 * blocks)
                gp.sem_inc(rows_free, 1)

            for g in range(NB + 2):
                next_slots(g)
                if g >= 2:
                    scatter(g, 4, 2 * g)
                gather_next(g)
                if g >= 2:
                    stored(g - 1)
                if g == 0:
                    over_experts()
                elif g <= NB:
                    over_slots(g - 1)
                else:
                    over_selectors()
            with gp.Fori(NB + 1, but_one) as before:
                g = before + 1
                next_slots(g)
                scatter(g, 4, 2 * before + 2)
                gather_next(g)
                stored(before)
            scatter(nblk, 4, 2 * nblk)
            stored(but_one)
            scatter(nblk, 3, 2 * nblk + 2)


INS = ["x", "norm1_g", "w_in", "q_norm_g", "k_norm_g", "rel_bias", "conv_w", "w_branch_conv", "w_branch_attn",
       "w_out", "norm2_g", "w_router", "b_router", "w_gate_up", "b_gate_up", "w_down", "b_down"]


def kernel(**inputs):
    import concourse.bacc as bacc
    from concourse.bass_utils import run_bass_kernel_spmd

    nc = bacc.Bacc("TRN2", target_bir_lowering=False, num_devices=1)
    arrays, args = {}, []
    given = {name: np.ascontiguousarray(inputs[name]) for name in INS}
    given["consts"] = constants()
    given["buckets"] = bucket_rows()
    for name, a in given.items():
        arrays[f"in_{name}"] = a
        args.append(nc.dram_tensor(f"in_{name}", a.shape, mybir.dt.from_np(a.dtype), kind="ExternalInput").ap())
    args.append(nc.dram_tensor("out", (1, S, D), F32, kind="ExternalOutput").ap())
    hybrid_block(nc, *args)
    r = run_bass_kernel_spmd(nc, [arrays], core_ids=[0])
    return r.results[0]["out"]
```
